# Optimizing a Trainium2 kernel written in Bass

```python
import math
import jax, jax.numpy as jnp
from jax import lax
import numpy as np

D_MODEL = 1024
BATCH = 1
SEQ = 128
DEPTH = 2
DEC_BATCH = 1
DEC_SEQ = 512
PAST_LEN = 128

GRID_W = 64
HEAD_DIM = 64
N_HEADS_A = 8
N_KV_A = 2
N_HEADS_B = 8
N_KV_B = 2
A_WIDTH = N_HEADS_A * HEAD_DIM
B_WIDTH = N_HEADS_B * HEAD_DIM
KV_WIDTH_A = N_KV_A * HEAD_DIM
KV_WIDTH_B = N_KV_B * HEAD_DIM
C_WIDTH = 512
C_GROUPS = 4
C_GROUP_DIM = C_WIDTH // C_GROUPS
CHUNK = 128
BLOCK = 128
WINDOW = 128
N_BRANCH = 3
IN_WIDTH = 2 * A_WIDTH + 2 * KV_WIDTH_A + 2 * B_WIDTH + 2 * KV_WIDTH_B + 3 * C_WIDTH
ROPE_BASE = 10000.0
ROPE_FREQS = HEAD_DIM // 4
EPS = 1e-6
NEG_INF = -1e30
DEEPNORM_ALPHA = (2 * DEPTH) ** 0.25
DEEPNORM_BETA = (8 * DEPTH) ** -0.25

kernel_name = 'hybrid_flow_prefix_trunk_step'

def layer_norm(x, g=None, b=None):
    xf = x.astype(jnp.float32)
    mu = jnp.mean(xf, axis=-1, keepdims=True)
    var = jnp.mean(jnp.square(xf - mu), axis=-1, keepdims=True)
    y = (xf - mu) * lax.rsqrt(var + EPS)
    if g is not None:
        y = y * g.astype(jnp.float32) + b.astype(jnp.float32)
    return y.astype(x.dtype)

def rms_norm(x, g):
    xf = x.astype(jnp.float32)
    y = xf * lax.rsqrt(jnp.mean(jnp.square(xf), axis=-1, keepdims=True) + EPS) * g.astype(jnp.float32)
    return y.astype(x.dtype)

def axial_rope_tables(n_tokens):
    rows = n_tokens // GRID_W
    row = jnp.repeat(jnp.arange(rows, dtype=jnp.float32), GRID_W)
    col = jnp.tile(jnp.arange(GRID_W, dtype=jnp.float32), rows)
    inv_freq = jnp.power(ROPE_BASE, -jnp.arange(ROPE_FREQS, dtype=jnp.float32) / ROPE_FREQS)
    ang = jnp.concatenate([row[:, None] * inv_freq, col[:, None] * inv_freq], axis=-1)
    return jnp.cos(ang), jnp.sin(ang)

def apply_rope(x, cos, sin):
    half = HEAD_DIM // 2
    xf = x.astype(jnp.float32)
    x1, x2 = xf[..., :half], xf[..., half:]
    c = cos[None, :, None, :]
    s = sin[None, :, None, :]
    return jnp.concatenate([x1 * c - x2 * s, x2 * c + x1 * s], axis=-1).astype(x.dtype)

def ada_modulation(cvec, w_mod, b_mod):
    m = (jax.nn.silu(cvec) @ w_mod + b_mod)[..., None, :]
    shift, scale, gate = jnp.split(m, 3, axis=-1)
    return shift, scale, gate

def split_projection(p):
    B, T, _ = p.shape
    sizes = [A_WIDTH, KV_WIDTH_A, KV_WIDTH_A, A_WIDTH,
             B_WIDTH, KV_WIDTH_B, KV_WIDTH_B, B_WIDTH,
             C_WIDTH, C_WIDTH, C_WIDTH]
    qa, ka, va, ga, qb, kb, vb, gb, uc, vc, gc = jnp.split(p, np.cumsum(sizes)[:-1].tolist(), axis=-1)
    heads = lambda t, n: t.reshape(B, T, n, HEAD_DIM)
    return dict(qa=heads(qa, N_HEADS_A), ka=heads(ka, N_KV_A), va=heads(va, N_KV_A), ga=ga,
                qb=heads(qb, N_HEADS_B), kb=heads(kb, N_KV_B), vb=heads(vb, N_KV_B), gb=gb,
                uc=uc, vc=vc, gc=gc)

def dense_gqa(q, k, v, n_kv, sink=None):
    B, T, H, d = q.shape
    G = H // n_kv
    nb = T // BLOCK
    qb = (q * d ** -0.5).reshape(B, nb, BLOCK, n_kv, G, d).transpose(1, 0, 2, 3, 4, 5)

    def one_block(qblk):
        s = jnp.einsum('bqkgd,blkd->bkgql', qblk, k).astype(jnp.float32)
        if sink is not None:
            col = jnp.broadcast_to(sink.astype(jnp.float32).reshape(n_kv, G)[:, :, None, None], s.shape[:-1] + (1,))
            s = jnp.concatenate([s, col], axis=-1)
        p = jax.nn.softmax(s, axis=-1)
        if sink is not None:
            p = p[..., :-1]
        return jnp.einsum('bkgql,blkd->bqkgd', p.astype(v.dtype), v)

    o = lax.map(one_block, qb)
    return o.transpose(1, 0, 2, 3, 4, 5).reshape(B, T, H, d)

def window_gqa(q, k, v, k_ctx, v_ctx, sink):
    B, N, H, d = q.shape
    G = H // N_KV_B
    nb = N // BLOCK
    P = k_ctx.shape[1]
    qb = (q * d ** -0.5).reshape(B, nb, BLOCK, N_KV_B, G, d)
    pad = ((0, 0), (WINDOW, WINDOW), (0, 0), (0, 0))

    def bands(t):
        tp = jnp.pad(t, pad).reshape(B, nb + 2, BLOCK, N_KV_B, d)
        return jnp.concatenate([tp[:, :-2], tp[:, 1:-1], tp[:, 2:]], axis=2)

    kband, vband = bands(k), bands(v)
    nband = 3 * BLOCK
    s_band = jnp.einsum('bnqkgd,bnlkd->bnkgql', qb, kband).astype(jnp.float32)
    blk = jnp.arange(nb)[:, None, None] * BLOCK
    q_pos = blk + jnp.arange(BLOCK)[None, :, None]
    k_pos = blk - WINDOW + jnp.arange(nband)[None, None, :]
    valid = (jnp.abs(q_pos - k_pos) <= WINDOW) & (k_pos >= 0) & (k_pos < N)
    s_band = jnp.where(valid[None, :, None, None], s_band, NEG_INF)
    s_ctx = jnp.einsum('bnqkgd,blkd->bnkgql', qb, k_ctx).astype(jnp.float32)
    s_sink = jnp.broadcast_to(sink.astype(jnp.float32).reshape(N_KV_B, G)[:, :, None, None], s_ctx.shape[:-1] + (1,))
    p = jax.nn.softmax(jnp.concatenate([s_band, s_ctx, s_sink], axis=-1), axis=-1)
    p_band = p[..., :nband].astype(v.dtype)
    p_ctx = p[..., nband:nband + P].astype(v.dtype)
    o = (jnp.einsum('bnkgql,bnlkd->bnqkgd', p_band, vband)
         + jnp.einsum('bnkgql,blkd->bnqkgd', p_ctx, v_ctx))
    return o.reshape(B, N, H, d)

def chunk_sgu(u, v, g, b, w_s, b_s):
    B, T, _ = v.shape
    vn = layer_norm(v, g, b).reshape(B, T // CHUNK, CHUNK, C_GROUPS, C_GROUP_DIM)
    mixed = jnp.einsum('gpq,bnqgc->bnpgc', w_s, vn) + b_s.T[:, :, None]
    return u * mixed.reshape(B, T, C_WIDTH)

def merge_and_residual(x, h, gate, br, a_out, b_out, c_out, lw):
    B, T, _ = x.shape
    ya = (a_out.reshape(B, T, A_WIDTH) * jax.nn.silu(br['ga'])) @ lw['w_proj_a']
    yb = (b_out.reshape(B, T, B_WIDTH) * jax.nn.silu(br['gb'])) @ lw['w_proj_b']
    yc = (c_out * jax.nn.silu(br['gc'])) @ lw['w_proj_c']
    g_a, g_b, g_c = jnp.split(jax.nn.sigmoid(h @ lw['w_gate'] + lw['b_gate']), N_BRANCH, axis=-1)
    y = (g_a * ya + g_b * yb + g_c * yc) @ lw['w_out']
    return layer_norm(DEEPNORM_ALPHA * x + gate * y, lw['ln_g'], lw['ln_b'])

def context_layer(x, c_ctx, lw):
    shift, scale, gate = ada_modulation(c_ctx, lw['w_mod'], lw['b_mod'])
    h = layer_norm(x) * (1 + scale) + shift
    br = split_projection(h @ lw['w_in'])
    qa = rms_norm(br['qa'], lw['q_norm'])
    ka = rms_norm(br['ka'], lw['k_norm'])
    a_out = dense_gqa(qa, ka, br['va'], N_KV_A)
    b_out = dense_gqa(br['qb'], br['kb'], br['vb'], N_KV_B, lw['sink'])
    c_out = chunk_sgu(br['uc'], br['vc'], lw['sgu_g'], lw['sgu_b'], lw['w_spatial'], lw['b_spatial'])
    x_new = merge_and_residual(x, h, gate, br, a_out, b_out, c_out, lw)
    return x_new, ka, br['va'], br['kb'], br['vb']

def latent_layer(x, c, lw, ka_ctx, va_ctx, kb_ctx, vb_ctx, cos, sin):
    shift, scale, gate = ada_modulation(c, lw['w_mod'], lw['b_mod'])
    h = layer_norm(x) * (1 + scale) + shift
    br = split_projection(h @ lw['w_in'])
    qa = apply_rope(rms_norm(br['qa'], lw['q_norm']), cos, sin)
    ka = apply_rope(rms_norm(br['ka'], lw['k_norm']), cos, sin)
    a_out = dense_gqa(qa, jnp.concatenate([ka, ka_ctx], axis=1),
                      jnp.concatenate([br['va'], va_ctx], axis=1), N_KV_A)
    qb = apply_rope(br['qb'], cos, sin)
    kb = apply_rope(br['kb'], cos, sin)
    b_out = window_gqa(qb, kb, br['vb'], kb_ctx, vb_ctx, lw['sink'])
    c_out = chunk_sgu(br['uc'], br['vc'], lw['sgu_g'], lw['sgu_b'], lw['w_spatial'], lw['b_spatial'])
    return merge_and_residual(x, h, gate, br, a_out, b_out, c_out, lw)

def setup_inputs(seed: int = 0) -> dict:
    key = jax.random.key(seed)
    ks = jax.random.split(key, 32)
    nrm = lambda k, shape, s: jax.random.normal(k, shape, jnp.float32) * s
    D = D_MODEL
    cache_shape = (DEC_BATCH, DEPTH, PAST_LEN, N_KV_A, HEAD_DIM)
    return {
        'x_prompt': nrm(ks[0], (BATCH, SEQ, D), 1.0),
        'x_sample': nrm(ks[1], (DEC_BATCH, DEC_SEQ, D), 1.0),
        'cache_a_k': nrm(ks[2], cache_shape, 1.0),
        'cache_a_v': nrm(ks[3], cache_shape, 1.0),
        'cache_b_k': nrm(ks[4], (DEC_BATCH, DEPTH, PAST_LEN, N_KV_B, HEAD_DIM), 1.0),
        'cache_b_v': nrm(ks[5], (DEC_BATCH, DEPTH, PAST_LEN, N_KV_B, HEAD_DIM), 1.0),
        'c': nrm(ks[6], (DEC_BATCH, D), 1.0),
        'c_ctx': nrm(ks[7], (D,), 1.0),
        'w_mod': nrm(ks[8], (DEPTH, D, 3 * D), D ** -0.5),
        'b_mod': nrm(ks[9], (DEPTH, 3 * D), 0.02),
        'w_in': nrm(ks[10], (DEPTH, D, IN_WIDTH), D ** -0.5),
        'q_norm': 1.0 + nrm(ks[11], (DEPTH, HEAD_DIM), 0.02),
        'k_norm': 1.0 + nrm(ks[12], (DEPTH, HEAD_DIM), 0.02),
        'sink': nrm(ks[13], (DEPTH, N_HEADS_B), 0.5),
        'sgu_g': 1.0 + nrm(ks[14], (DEPTH, C_WIDTH), 0.02),
        'sgu_b': nrm(ks[15], (DEPTH, C_WIDTH), 0.02),
        'w_spatial': nrm(ks[16], (DEPTH, C_GROUPS, CHUNK, CHUNK), CHUNK ** -0.5),
        'b_spatial': nrm(ks[17], (DEPTH, C_GROUPS, CHUNK), 0.02),
        'w_proj_a': nrm(ks[18], (DEPTH, A_WIDTH, D), A_WIDTH ** -0.5 * DEEPNORM_BETA),
        'w_proj_b': nrm(ks[19], (DEPTH, B_WIDTH, D), B_WIDTH ** -0.5 * DEEPNORM_BETA),
        'w_proj_c': nrm(ks[20], (DEPTH, C_WIDTH, D), C_WIDTH ** -0.5 * DEEPNORM_BETA),
        'w_gate': nrm(ks[21], (DEPTH, D, N_BRANCH * D), D ** -0.5),
        'b_gate': nrm(ks[22], (DEPTH, N_BRANCH * D), 0.02),
        'w_out': nrm(ks[23], (DEPTH, D, D), D ** -0.5 * DEEPNORM_BETA),
        'ln_g': 1.0 + nrm(ks[24], (DEPTH, D), 0.02),
        'ln_b': nrm(ks[25], (DEPTH, D), 0.02),
    }

def reference(x_prompt, x_sample, cache_a_k, cache_a_v, cache_b_k, cache_b_v, c, c_ctx,
              w_mod, b_mod, w_in, q_norm, k_norm, sink, sgu_g, sgu_b, w_spatial, b_spatial,
              w_proj_a, w_proj_b, w_proj_c, w_gate, b_gate, w_out, ln_g, ln_b):
    cos, sin = axial_rope_tables(x_sample.shape[1])
    xp, xs = x_prompt, x_sample
    ka_l, va_l, kb_l, vb_l = [], [], [], []
    for l in range(DEPTH):
        lw = dict(w_mod=w_mod[l], b_mod=b_mod[l], w_in=w_in[l], q_norm=q_norm[l], k_norm=k_norm[l],
                  sink=sink[l], sgu_g=sgu_g[l], sgu_b=sgu_b[l], w_spatial=w_spatial[l],
                  b_spatial=b_spatial[l], w_proj_a=w_proj_a[l], w_proj_b=w_proj_b[l],
                  w_proj_c=w_proj_c[l], w_gate=w_gate[l], b_gate=b_gate[l], w_out=w_out[l],
                  ln_g=ln_g[l], ln_b=ln_b[l])
        xp, ka, va, kb, vb = context_layer(xp, c_ctx, lw)
        ka_l.append(ka)
        va_l.append(va)
        kb_l.append(kb)
        vb_l.append(vb)
        xs = latent_layer(xs, c, lw, cache_a_k[:, l], cache_a_v[:, l], cache_b_k[:, l], cache_b_v[:, l], cos, sin)
    state_a_k = jnp.stack(ka_l, axis=1)
    state_a_v = jnp.stack(va_l, axis=1)
    state_b_k = jnp.stack(kb_l, axis=1)
    state_b_v = jnp.stack(vb_l, axis=1)
    return (xp, xs, state_a_k, state_a_v, state_b_k, state_b_v)


_drawn_inputs = setup_inputs


def setup_inputs(seed=0):
    import zlib

    import numpy as np

    out = dict(_drawn_inputs(seed))
    spreads = {}
    factors = {'cache_a_k': 8.0,
     'cache_a_v': 8.0,
     'cache_b_k': 8.0,
     'cache_b_v': 8.0,
     'q_norm': 8.0,
     'k_norm': 9.53,
     'sink': 59.109,
     'sgu_g': 24.467,
     'sgu_b': 24.123,
     'b_spatial': 23.631,
     'b_gate': 8.0}
    for name, (base, spread) in spreads.items():
        noise = np.random.default_rng([zlib.crc32(name.encode()), seed]).standard_normal(out[name].shape)
        drawn = base * np.exp(spread * noise) if base else spread * noise
        out[name] = __import__('jax').numpy.asarray(drawn.astype(out[name].dtype))
    for name, factor in factors.items():
        out[name] = (out[name] * factor).astype(out[name].dtype)
    return out
```

```python
from contextlib import ExitStack

import numpy as np

import concourse.bass as bass
from concourse import mybir

P = 128
F32 = mybir.dt.float32
F32R = mybir.dt.float32r
ALU = mybir.AluOpType
ACT = mybir.ActivationFunctionType
AX = mybir.AxisListType

D = 1024
DEPTH = 2
T = 5
TOK = T * P
HALF = TOK // 2
HD = 64
NKV = 2
GRP = 4
KT_D = D // P
BW = 512
KT_B = BW // P
COLS = 256
UK = 4
RAW = 3
RING = 5
EPS = 1e-6
ALPHA = (2 * DEPTH) ** 0.25
NEG = -1e30
SLOTS = 4
CACHE = T

KV_GROUP = {"a": 2, "b": 7}
Q_GROUP = {"a": (0, 1), "b": (5, 6)}
G_GROUP = {"a": (3, 4), "b": (8, 9)}
U_GROUP, V_GROUP, GC_GROUP = (10, 11), (12, 13), (14, 15)
QUERY_TILES = (1, 2, 3, 4, 0)


def key_slots(branch, tile):
    if tile == 0:
        return [(0, None)]
    if branch == "a":
        return [(s, None) for s in (1, 2, 3, 4, CACHE)]
    band = [(s, {-1: "before", 0: None, 1: "after"}[s - tile]) for s in (tile - 1, tile, tile + 1) if 1 <= s < T]
    return band + [(CACHE, None)]


def layer_order():
    units, order, last_use = [], [], {}

    def group(kind, index, rows, col, entries):
        first = len(units)
        for k0 in range(0, rows, UK):
            units.append((kind, index, k0, col))
        order.extend(entries)
        return first

    for b in range(8):
        units.extend([("mod", 0, 0, b * COLS), ("mod", 0, UK, b * COLS)])
        order.append(("mod", b))
    order.append(("cols",))
    order += [("h", j) for j in range(KT_D)]

    split_units = []
    uses = {}

    def use(kind, index, rows, col):
        mine = []
        for k0 in range(0, rows, UK):
            units.append((kind, index, k0, col))
            mine.append(len(split_units))
            split_units.append(len(units) - 1)
        return mine

    def dense(groups):
        behind = []
        for g in groups:
            mine = use("in", 0, KT_D, g * COLS)
            for t in range(T):
                order.append(("in", g, t))
                for kind, br, kv in behind[:]:
                    pass
                uses[("in", g, t)] = mine
                pend.append((g, t))
                if len(pend) > 2:
                    transposes(*pend.pop(0))
            for u in mine:
                last_use[u] = ("in", g, T - 1)

    def transposes(g, t):
        for br in "ab":
            if g == KV_GROUP[br]:
                order.append(("kt", br, t))
                if t == T - 1:
                    order.append(("kt", br, CACHE))
            if g in Q_GROUP[br]:
                order.append(("qt", br, Q_GROUP[br].index(g), t))

    def flush():
        while pend:
            transposes(*pend.pop(0))

    def attention(br, kv):
        n = GRP * T
        for i in (0, 1):
            order.append(("s", br, kv, i))
        for i in range(n + 3):
            if i < n:
                order.append(("pt", br, kv, i))
            if 1 <= i <= n:
                order.append(("pv", br, kv, i - 1))
            if i + 2 < n:
                order.append(("s", br, kv, i + 2))
            if i >= GRP + 1 and (i - 2) % GRP == GRP - 1:
                order.append(("ot", br, kv, (i - 2) // GRP))

    def gates(r):
        for g in range(D // COLS):
            gate = use("gate", 0, KT_D, r * D + g * COLS)
            proj = use("proj", r, KT_B, g * COLS)
            for j in (2 * g, 2 * g + 1):
                order.append(("z", r, j))
                order.append(("y", r, j))
                uses[("z", r, j)] = gate
                uses[("y", r, j)] = proj
            for u in gate + proj:
                last_use[u] = ("y", r, 2 * g + 1)
            if r == 2:
                order.append(("mod", 8 + g))

    pend = []
    for r, br in enumerate("ab"):
        dense((KV_GROUP[br], Q_GROUP[br][0], G_GROUP[br][0]))
        flush()
        attention(br, 0)
        dense((Q_GROUP[br][1], G_GROUP[br][1]))
        flush()
        attention(br, 1)
        gates(r)
    dense(V_GROUP + GC_GROUP + U_GROUP)
    pend.clear()
    for g in range(KT_B):
        order.append(("mix", g))
        if g:
            order.append(("ct", g - 1))
    order.append(("ct", KT_B - 1))
    gates(2)
    order += [("m", j) for j in range(KT_D)]
    for g in range(D // COLS):
        mine = use("out", 0, KT_D, g * COLS)
        for t in range(T):
            order.append(("out", g, t))
            uses[("out", g, t)] = mine
        for u in mine:
            last_use[u] = ("out", g, T - 1)

    full = []
    early = {0: [0, 1], 3: [2], 5: [3], 7: [4]}
    after = {}
    for n in range(RING, len(split_units)):
        after.setdefault(last_use[n - RING], []).append(n)
    for e in order:
        full.append(e)
        if e[0] == "cols":
            full += [("split", n) for n in early[0]]
        if e[0] == "h":
            full += [("split", n) for n in early.get(e[1], []) if e[1] > 0 and n < RING]
        full += [("split", n) for n in after.get(e, [])]
    return full, units, split_units, uses, last_use


ORDER, UNITS, SPLIT_UNITS, USES, LAST_USE = layer_order()


def slot_plan():
    place, count, turn = {}, [0] * SLOTS, 0

    def take(key, s):
        place[key] = (s, count[s])
        count[s] += 1

    for e in ORDER:
        kind = e[0]
        if kind in ("mod", "cols", "h", "in", "kt", "qt", "z", "y", "mix", "ct", "out"):
            take(e, turn % SLOTS)
            turn += 1
            if kind == "mod" and e[1] >= 8:
                take(("bc", e[1]), turn % SLOTS)
                turn += 1
        elif kind == "s":
            if e[3] == 0:
                turn = 0
            take(e, e[3] % 2)
    return place


PLACE = slot_plan()


def build(nc, a, outs):
    with ExitStack() as ctx:
        def sb(name, shape, dt=F32):
            return ctx.enter_context(nc.sbuf_tensor(name, shape, dt))

        def sem(name):
            return ctx.enter_context(nc.semaphore(name))

        x = sb("x", [P, T, D])
        h_hi, h_lo = sb("h_hi", [P, KT_D, TOK], F32R), sb("h_lo", [P, KT_D, TOK], F32R)
        o_hi, o_lo = sb("o_hi", [P, KT_B, TOK], F32R), sb("o_lo", [P, KT_B, TOK], F32R)
        w_hi, w_lo = sb("w_hi", [P, RING, UK, COLS], F32R), sb("w_lo", [P, RING, UK, COLS], F32R)
        raw = sb("raw", [P, RAW, UK, COLS])
        ident = sb("ident", [P, P])
        ident_r = sb("ident_r", [P, P], F32R)
        mask_r = sb("mask_r", [P, 2, P], F32R)
        pick = sb("pick", [P, 2, P])
        silu_c = sb("silu_c", [P, KT_D, 32])
        c_in = sb("c_in", [P, 2, KT_D])
        rope = sb("rope", [P, T - 1, 2, HD])
        norm = sb("norm", [P, 2, 2, HD])
        table = sb("table", [P, 2, T - 1, 2, HD])
        sink = sb("sink", [P, 2 * GRP])
        b_mod_col = sb("b_mod_col", [P, 2 * KT_D])
        b_gate_col = sb("b_gate_col", [P, 3 * KT_D])
        b_sp_col = sb("b_sp_col", [P, KT_B])
        w_sp_t = sb("w_sp_t", [P, KT_B, P])
        cache_k = sb("cache_k", [P, 2, NKV, 2, HD])
        k_st = sb("k_st", [P, 3, NKV, 2, HD])
        cache_v = sb("cache_v", [P, 2, P])
        ada = sb("ada", [P, 2 * KT_D, 2])
        bn = sb("bn", [P, T, 2, 6])
        mv = sb("mv", [P, T, 2])
        rstd = sb("rstd", [P, T])
        nmr = sb("nmr", [P, T])
        with_eps = sb("with_eps", [P, 8])
        minus_half = sb("minus_half", [P, 8])
        ssq = sb("ssq", [P, 2, GRP])
        rqk = sb("rqk", [P, 2, GRP])
        top = sb("top", [P, 2 * GRP])
        neg_top = sb("neg_top", [P, 2 * GRP])
        psums = sb("psums", [P, 2 * GRP])
        psink = sb("psink", [P, 2 * GRP])
        rinv = sb("rinv", [P, 2, GRP])

        at0 = (nc.sbuf_base + 63) // 64 * 64
        MERGE = 20480
        ARENA = 42496
        nc_slab = sb("phase_memory", [P, (MERGE + ARENA + 64) // 4])
        assert nc_slab is not None

        def at(name, offset, shape, dt=F32):
            size = int(np.prod(shape[1:])) * 4
            assert offset + size <= MERGE + ARENA, name
            return nc.alloc_sbuf_tensor_at(name, shape, dt, offset=at0 + offset)

        merge = at("merge", 0, [P, KT_D, TOK])
        xn = at("xn", 0, [P, T, D])
        A0 = MERGE
        mod_rows = at("mod_rows", A0, [P, 2 * D])
        hf = at("hf", A0 + 10240, [P, 2, TOK])
        wsp_in = at("wsp_in", A0 + 16384, [P, KT_B, P])
        q_t = at("q_t", A0, [P, GRP, TOK], F32R)
        k_hi = at("k_hi", A0 + 10240, [P, NKV, TOK + P], F32R)
        k_lo = at("k_lo", A0 + 16384, [P, NKV, TOK + P], F32R)
        vals = at("vals", A0 + 22528, [P, T, P])
        gate_br = at("gate_br", A0 + 25088, [P, T, COLS])
        square = at("square", A0 + 30208, [P, 2, COLS])
        rot_c = at("rot_c", A0 + 32256, [P, 2, COLS])
        rot_s = at("rot_s", A0 + 34304, [P, 2, COLS])
        q_st = at("q_st", A0 + 36352, [P, 2, COLS])
        prob = at("prob", A0 + 30208, [P, 2, 5 * P])
        prob_t = at("prob_t", A0 + 35328, [P, 2, 5, P])
        og = at("og", A0 + 40448, [P, 2, COLS])
        vn = at("vn", A0, [P, T, BW])
        ug = at("ug", A0 + 10240, [P, T, BW])
        sgu_g = at("sgu_g", A0 + 20480, [P, BW])
        sgu_b = at("sgu_b", A0 + 22528, [P, BW])
        sg = at("sg", A0 + 31232, [P, 2, TOK])
        gy = at("gy", A0 + 36352, [P, 2, TOK])
        mod_raw = at("mod_raw", A0, [P, 2, UK, COLS])
        gate_bc = at("gate_bc", A0 + 8192, [P, 2, D])
        ln_g_bc = at("ln_g_bc", A0 + 16384, [P, D])
        ln_b_bc = at("ln_b_bc", A0 + 20480, [P, D])
        gate_rows = at("gate_rows", A0 + 24576, [P, 2, COLS])
        b_modg_bc = at("b_modg_bc", A0 + 26624, [P, D])
        scaled = at("scaled", A0 + 31232, [P, 2, COLS])

        ps = ctx.enter_context(nc.psum_tensor("ps", [P, 2 * SLOTS, 512], F32))

        def slot(s):
            return ps[:, 2 * s:2 * s + 2, :].rearrange("p b n -> p (b n)")

        loaded = sem("loaded")
        consts = sem("consts")
        setup = sem("setup")
        params = sem("params")
        late = sem("late")
        ends = sem("ends")
        raw_full = [sem(f"raw_full{i}") for i in range(RAW)]
        mod_half = sem("mod_half")
        modg_in = sem("modg_in")
        hi_made = sem("hi_made")
        w_ready = sem("w_ready")
        filled = [sem(f"filled{i}") for i in range(SLOTS)]
        drained = [sem(f"drained{i}") for i in range(SLOTS)]
        var_ready, rstd_ready = sem("var_ready"), sem("rstd_ready")
        xn_ready, hh_ready, h_ready = sem("xn_ready"), sem("hh_ready"), sem("h_ready")
        wsp_ready = sem("wsp_ready")
        sq_ready, staged = sem("sq_ready"), sem("staged")
        t_hi = sem("t_hi")
        nm_ready = sem("nm_ready")
        sink_exp = sem("sink_exp")
        p_turned = sem("p_turned")
        pt_a, pt_b = sem("pt_a"), sem("pt_b")
        o_full, o_used = sem("o_full"), sem("o_used")
        og_ready, ot_full, ot_done = sem("og_ready"), sem("ot_full"), sem("ot_done")
        vn_in, vn_ready = sem("vn_in"), sem("vn_ready")
        mixed = sem("mixed")
        rows_ready = sem("rows_ready")
        gy_ready, merged = sem("gy_ready"), sem("merged")
        m_hi, m_ready = sem("m_hi"), sem("m_ready")
        y_done, nmr_ready, x_normed, x_scaled, x_done = (sem(n) for n in ("y_done", "nmr_ready", "x_normed", "x_scaled", "x_done"))
        state_out = sem("state_out")
        pe_step, act_step, dve_step, pool_step = (sem(n) for n in ("pe_step", "act_step", "dve_step", "pool_step"))
        final = sem("final")
        per_layer = [params, late, ends, *raw_full, mod_half, modg_in, hi_made, w_ready, *filled, *drained, var_ready,
                     rstd_ready, xn_ready, hh_ready, h_ready, wsp_ready, sq_ready, staged, t_hi, nm_ready,
                     sink_exp, p_turned, pt_a, pt_b, o_full, o_used, og_ready, ot_full, ot_done, vn_in, vn_ready,
                     mixed, rows_ready, gy_ready, merged, m_hi, m_ready, y_done, nmr_ready, x_normed, x_scaled,
                     x_done, state_out, pe_step, act_step, dve_step, pool_step]

        class Tally:

            def __init__(self, eng, step):
                self.eng, self.step, self.n = eng, step, {}

            def did(self, instruction, semaphore=None):
                s = semaphore or self.step
                instruction.then_inc(s, 1)
                self.n[s.name] = self.n.get(s.name, 0) + 1
                return s, self.n[s.name]

            def count(self, semaphore):
                return self.n.get(semaphore.name, 0)

        def wait_filled(eng, stage):
            s, k = PLACE[stage]
            eng.wait_ge(filled[s], k + 1)
            return s

        def wait_drained(eng, stage):
            s, k = PLACE[stage]
            eng.wait_ge(drained[s], k + 1)

        def raw_at(n):
            return n % RAW, 16 * (n // RAW + 1)

        with nc.Block() as block:
            @block.sync
            def _(sp):
                sp.dma_start(x[:, 0, :], a["x_prompt"][0]).then_inc(loaded, 16)
                for t in range(1, T):
                    sp.dma_start(x[:, t, :], a["x_sample"][0, (t - 1) * P:t * P, :]).then_inc(loaded, 16)

            @block.scalar
            def _(act):
                act.dma_start(c_in[:, 0, :], a["c_ctx"].rearrange("(j p) -> p j", p=P), allow_slow_non_contiguous=True).then_inc(setup, 16)
                act.dma_start(c_in[:, 1, :], a["c"][0].rearrange("(j p) -> p j", p=P), allow_slow_non_contiguous=True).then_inc(setup, 16)
                act.dma_start(rope[:, :, :, :], a["rope"]).then_inc(loaded, 16)
                act.wait_ge(setup, 32)
                act.wait_ge(consts, 1)
                act.activation(silu_c[:, :, 0:2], c_in[:, :, :].rearrange("p s j -> p j s"), ACT.Silu).then_inc(act_step, 1)
                act.wait_ge(act_step, 1)

            @block.gpsimd
            def _(pool):
                mine = [0]

                def step(ins):
                    mine[0] += 1
                    ins.then_inc(consts, 1)
                    pool.wait_ge(consts, mine[0])

                step(pool.memset(silu_c[:, :, :], 0.0))
                step(pool.memset(minus_half[:, :], -0.5))
                step(pool.memset(ident[:, :], 0.0))
                step(pool.affine_select(out=ident[:, :], in_=ident[:, :], compare_op=ALU.not_equal, fill=1.0,
                                        base=0, pattern=[[-1, P]], channel_multiplier=1))
                step(pool.memset(pick[:, :, :], 0.0))
                for s in range(2):
                    for g in range(4):
                        step(pool.affine_select(out=pick[:, s, :], in_=pick[:, s, :], compare_op=ALU.not_equal,
                                                fill=1.0, base=-(32 * g + s), pattern=[[0, P]], channel_multiplier=1))
                step(pool.memset(hf[:, 0, 0:2 * P], 0.0))
                step(pool.affine_select(out=hf[:, 0, 0:P], in_=hf[:, 0, 0:P], compare_op=ALU.is_ge, fill=NEG,
                                        base=0, pattern=[[1, P]], channel_multiplier=-1))
                step(pool.affine_select(out=hf[:, 0, P:2 * P], in_=hf[:, 0, P:2 * P], compare_op=ALU.is_ge, fill=NEG,
                                        base=0, pattern=[[-1, P]], channel_multiplier=1))

            @block.vector
            def _(dve):
                dve.wait_ge(consts, 16)
                dve.tensor_copy(ident_r[:, :], ident[:, :]).then_inc(dve_step, 1)
                dve.tensor_copy(mask_r[:, :, :].rearrange("p s n -> p (s n)"), hf[:, 0, 0:2 * P]).then_inc(dve_step, 1)
                dve.wait_ge(dve_step, 2)
                dve.wait_ge(loaded, 16 * (T + 1))

        with nc.Fori(0, DEPTH) as layer:
            for s in per_layer:
                nc.sync.sem_clear(s)
            nc.all_engine_barrier()
            w_of = {"mod": a["w_mod"], "in": a["w_in"], "gate": a["w_gate"], "out": a["w_out"],
                    ("proj", 0): a["w_proj_a"], ("proj", 1): a["w_proj_b"], ("proj", 2): a["w_proj_c"]}
            N_UNITS_MAIN = len(UNITS)

            def of_layer(name):
                src = a[name]
                return src[(bass.ds(layer, 1),) + (slice(None),) * (len(src.shape) - 1)]

            def unit_source(kind, index, k0, col):
                w = w_of[(kind, index) if kind == "proj" else kind]
                rows = w[bass.ds(layer, 1), k0 * P:(k0 + UK) * P, col:col + COLS]
                return rows.rearrange("a (k p) n -> p (a k) n", p=P)

            with nc.Block() as block:
                def normalise(act, tally, t):
                    act.wait_ge(nmr_ready, t + 1)
                    tally.did(act.activation(x[:, t, :], x[:, t, :], ACT.Identity, bias=nmr[:, t:t + 1],
                                             scale=rstd[:, t:t + 1]), x_normed)

                def apply_ln_g(dve, did, t):
                    dve.wait_ge(x_normed, t + 1)
                    did(dve.tensor_tensor(x[:, t, :], x[:, t, :], ln_g_bc[:, :], ALU.mult), x_scaled)

                def add_ln_b(pool, did, t):
                    pool.wait_ge(x_scaled, t + 1)
                    did(pool.tensor_tensor(x[:, t, :], x[:, t, :], ln_b_bc[:, :], ALU.add), x_done)
                    if t == T - 1:
                        pool.wait_ge(x_done, T)

                @block.sync
                def _(sp):
                    for n in range(N_UNITS_MAIN):
                        r, full = raw_at(n)
                        if n >= RAW:
                            m = n - RAW
                            kind, _, k0, col = UNITS[m]
                            if kind == "mod" and k0 == 0:
                                sp.wait_ge(mod_half, col // COLS + 1)
                            elif kind == "mod":
                                wait_filled(sp, ("mod", col // COLS))
                            else:
                                sp.wait_ge(w_ready, SPLIT_UNITS.index(m) + 1)
                        sp.dma_start(raw[:, r, :, :], unit_source(*UNITS[n])).then_inc(raw_full[r], 16)

                @block.tensor
                def _(pe):
                    tally = Tally(pe, pe_step)

                    def begin(stage):
                        s, k = PLACE[stage]
                        if k:
                            pe.wait_ge(drained[s], k)
                        return s

                    def split_product(out, st_hi, st_lo, mv_hi, mv_lo, start, stop):
                        pe.matmul(out, st_hi, mv_hi, start=start, stop=False)
                        pe.matmul(out, st_hi, mv_lo, start=False, stop=False)
                        return pe.matmul(out, st_lo, mv_hi, start=False, stop=stop)

                    def ring(u, k):
                        return w_hi[:, u % RING, k, :], w_lo[:, u % RING, k, :]

                    def token_rows(stage, lhs_hi, lhs_lo, ready):
                        t = stage[2]
                        s = begin(stage)
                        mine = USES[stage]
                        for k in range(KT_D):
                            if t == 0:
                                if k % UK == 0:
                                    pe.wait_ge(w_ready, mine[k // UK] + 1)
                                if ready is not None:
                                    pe.wait_ge(ready, k + 1)
                            wh, wl = ring(mine[k // UK], k % UK)
                            last = split_product(slot(s)[:, 0:COLS], lhs_hi[:, k, t * P:(t + 1) * P],
                                                 lhs_lo[:, k, t * P:(t + 1) * P], wh, wl, k == 0, k == KT_D - 1)
                        tally.did(last, filled[s])

                    def channel_rows(stage, act_hi, act_lo, kt):
                        j = stage[2]
                        s = begin(stage)
                        mine = USES[stage]
                        c = (j % 2) * P
                        for k in range(kt):
                            if j % 2 == 0 and k % UK == 0:
                                pe.wait_ge(w_ready, mine[k // UK] + 1)
                            wh, wl = ring(mine[k // UK], k % UK)
                            for part, (w, acts) in enumerate(((wh, act_hi), (wh, act_lo), (wl, act_hi))):
                                for half in range(2):
                                    last = pe.matmul(ps[:, 2 * s + half, 0:HALF], w[:, c:c + P],
                                                     acts[:, k, half * HALF:(half + 1) * HALF],
                                                     start=k == 0 and part == 0, stop=k == kt - 1 and part == 2)
                        tally.did(last, filled[s])

                    def unit_of(i):
                        return QUERY_TILES[i // GRP], i % GRP

                    units_done = [0]

                    for e in ORDER:
                        kind = e[0]
                        if kind == "mod" and e[1] < 8:
                            s = begin(e)
                            for half in range(2):
                                r, full = raw_at(2 * e[1] + half)
                                pe.wait_ge(raw_full[r], full)
                                for k in range(UK):
                                    last = pe.matmul(slot(s)[32 * k:32 * k + 32, 0:COLS],
                                                     silu_c[:, half * UK + k, :], raw[:, r, k, :],
                                                     start=half == 0, stop=half == 1)
                                tally.did(last, filled[s] if half else mod_half)
                        elif kind == "mod":
                            g = e[1] - 8
                            s = begin(e)
                            pe.wait_ge(modg_in, 32 * (g + 1))
                            for half in range(2):
                                for k in range(UK):
                                    last = pe.matmul(slot(s)[32 * k:32 * k + 32, 0:COLS],
                                                     silu_c[:, half * UK + k, :], mod_raw[:, half, k, :],
                                                     start=half == 0, stop=half == 1)
                            tally.did(last, filled[s])
                            s = begin(("bc", e[1]))
                            wait_drained(pe, e)
                            for v in range(2):
                                last = pe.matmul(ps[:, 2 * s + v, 0:COLS], pick[:, v, :], gate_rows[:, g % 2, :],
                                                 start=True, stop=True)
                            tally.did(last, filled[s])
                        elif kind == "cols":
                            s = begin(e)
                            wait_drained(pe, ("mod", 7))
                            wait_drained(pe, ("mod", 6))
                            wait_drained(pe, ("mod", 5))
                            wait_drained(pe, ("mod", 4))
                            for n in range(2 * KT_D):
                                pe.matmul(slot(s)[:, 2 * n:2 * n + 2], mod_rows[:, n * P:(n + 1) * P],
                                          pick[:, :, 0], start=True, stop=True)
                            pe.wait_ge(wsp_ready, 16)
                            for g in range(KT_B):
                                last = pe.transpose(ps[:, 2 * s + 1, g * P:(g + 1) * P], wsp_in[:, g, :], ident[:, :])
                            tally.did(last, filled[s])
                        elif kind == "h":
                            s = begin(e)
                            if e[1] == 0:
                                pe.wait_ge(xn_ready, T)
                            for t in range(T):
                                last = pe.transpose(slot(s)[:, t * P:(t + 1) * P],
                                                    xn[:, t, e[1] * P:(e[1] + 1) * P], ident[:, :])
                            tally.did(last, filled[s])
                        elif kind == "in":
                            token_rows(e, h_hi, h_lo, h_ready if e[1] == KV_GROUP["a"] else None)
                        elif kind == "kt":
                            _, br, t = e
                            s = begin(e)
                            if t < T:
                                pe.wait_ge(staged, STAGED[("k", br, t)])
                            for kv in range(NKV):
                                if t == CACHE:
                                    src = cache_k[:, "ab".index(br), kv, :, :]
                                else:
                                    src = k_st[:, k_buffer(t), kv, :, :]
                                last = pe.transpose(slot(s)[:, kv * P:(kv + 1) * P],
                                                    src.rearrange("p d n -> p (d n)"), ident[:, :])
                            tally.did(last, filled[s])
                        elif kind == "qt":
                            _, br, kv, t = e
                            s = begin(e)
                            pe.wait_ge(staged, STAGED[("q", br, kv, t)])
                            for hh in range(GRP):
                                last = pe.transpose(slot(s)[0:HD, hh * P:(hh + 1) * P],
                                                    q_st[:, t % 2, hh * HD:(hh + 1) * HD], ident[:, :])
                            tally.did(last, filled[s])
                        elif kind == "s":
                            _, br, kv, i = e
                            if i == 0:
                                for q in range(SLOTS):
                                    before = slot_uses_before(e, q)
                                    if before:
                                        pe.wait_ge(drained[q], before)
                            s = begin(e)
                            t, hh = unit_of(i)
                            keys = key_slots(br, t)
                            runs = key_runs(keys)
                            q = q_t[:, hh, t * P:(t + 1) * P]
                            for col, width, src in runs:
                                masks = [(n, m) for n, (_, m) in enumerate(keys) if m and col <= n * P < col + width]
                                pe.matmul(slot(s)[:, col:col + width], q, k_hi[:, kv, src:src + width],
                                          start=True, stop=False)
                                last = pe.matmul(slot(s)[:, col:col + width], q, k_lo[:, kv, src:src + width],
                                                 start=False, stop=not masks)
                                for n, m in masks:
                                    last = pe.matmul(slot(s)[:, n * P:(n + 1) * P], ident_r[:, :],
                                                     mask_r[:, 0 if m == "before" else 1, :],
                                                     start=False, stop=(n, m) == masks[-1])
                            tally.did(last, filled[s])
                        elif kind == "pt":
                            _, br, kv, i = e
                            t, hh = unit_of(i)
                            keys = key_slots(br, t)
                            wait_drained(pe, ("s", br, kv, i))
                            waits = {pt_a: PT_COUNT[(br, kv, i)][0], pt_b: PT_COUNT[(br, kv, i)][1]}
                            for sm, n in waits.items():
                                if n:
                                    pe.wait_ge(sm, n)
                            first = pt_split(len(keys))
                            for n in range(len(keys)):
                                bank, col = (4, n) if n < first else (5, n - first)
                                last = pe.transpose(ps[:, bank, col * P:(col + 1) * P],
                                                    prob[:, i % 2, n * P:(n + 1) * P], ident[:, :])
                            tally.did(last, p_turned)
                        elif kind == "pv":
                            _, br, kv, i = e
                            t, hh = unit_of(i)
                            keys = key_slots(br, t)
                            na, nb = PT_COUNT[(br, kv, i)]
                            pe.wait_ge(pt_a, na + 1)
                            if len(keys) > pt_split(len(keys)):
                                pe.wait_ge(pt_b, nb + 1)
                            o = TILE_NO[(br, kv, i // GRP)]
                            if hh == 0 and o >= 2:
                                pe.wait_ge(ot_done, o - 1)
                            for n, (ks, _) in enumerate(keys):
                                v = cache_v[:, "ab".index(br), kv * HD:(kv + 1) * HD] if ks == CACHE \
                                    else vals[:, ks, kv * HD:(kv + 1) * HD]
                                last = pe.matmul(ps[:, 6 + o % 2, hh * HD:(hh + 1) * HD], prob_t[:, i % 2, n, :], v,
                                                 start=n == 0, stop=n == len(keys) - 1)
                            tally.did(last, o_full)
                        elif kind == "ot":
                            _, br, kv, j = e
                            o = TILE_NO[(br, kv, j)]
                            pe.wait_ge(og_ready, o + 1)
                            for c in range(2):
                                last = pe.transpose(ps[:, 6 + o % 2, c * P:(c + 1) * P],
                                                    og[:, o % 2, c * P:(c + 1) * P], ident[:, :])
                            tally.did(last, ot_full)
                        elif kind == "z":
                            channel_rows(e, h_hi, h_lo, KT_D)
                        elif kind == "y":
                            if e[2] == 0:
                                if e[1] < 2:
                                    pe.wait_ge(ot_done, TILE_NO[("ab"[e[1]], 1, T - 1)] + 1)
                                else:
                                    for g in range(KT_B):
                                        wait_drained(pe, ("ct", g))
                            channel_rows(e, o_hi, o_lo, KT_B)
                        elif kind == "mix":
                            g = e[1]
                            s = begin(e)
                            pe.wait_ge(vn_ready, T)
                            pe.matmul(slot(s)[:, 0:4 * P], w_sp_t[:, g, :], vn[:, 0:4, g * P:(g + 1) * P],
                                      start=True, stop=True)
                            last = pe.matmul(slot(s)[:, 4 * P:TOK], w_sp_t[:, g, :], vn[:, 4, g * P:(g + 1) * P],
                                             start=True, stop=True)
                            tally.did(last, filled[s])
                        elif kind == "ct":
                            g = e[1]
                            s = begin(e)
                            wait_drained(pe, ("mix", g))
                            for t in range(T):
                                last = pe.transpose(slot(s)[:, t * P:(t + 1) * P], ug[:, t, g * P:(g + 1) * P],
                                                    ident[:, :])
                            tally.did(last, filled[s])
                        elif kind == "out":
                            token_rows(e, h_hi, h_lo, m_ready if e[1] == 0 else None)

                @block.scalar
                def _(act):
                    tally = Tally(act, act_step)

                    def load(sm, dst, src, by_element=False):
                        act.dma_start(dst, src, allow_slow_non_contiguous=by_element).then_inc(sm, 16)

                    load(params, b_mod_col[:, :], of_layer("b_mod")[:, 0:2 * D].rearrange("a (j p) -> p (a j)", p=P), True)
                    load(wsp_ready, wsp_in[:, :, :], of_layer("w_spatial").rearrange("a g p q -> p (a g) q"))
                    for n, name in enumerate(("q_norm", "k_norm")):
                        row = of_layer(name)
                        load(params, norm[:, n, 0, :], row.to_broadcast([P, HD]))
                        load(params, norm[:, n, 1, 0:HD // 2], row[:, HD // 2:HD].to_broadcast([P, HD // 2]))
                        load(params, norm[:, n, 1, HD // 2:HD], row[:, 0:HD // 2].to_broadcast([P, HD // 2]))
                    load(params, sink[:, :], of_layer("sink").to_broadcast([P, 2 * GRP]))
                    for n, br in enumerate("ab"):
                        keys = a[f"cache_{br}_k"][0, bass.ds(layer, 1)].rearrange("a p h d -> p (a h) d")
                        vs = a[f"cache_{br}_v"][0, bass.ds(layer, 1)].rearrange("a p h d -> p (a h d)")
                        for dup in range(2):
                            load(params, cache_k[:, n, :, dup, :], keys)
                        load(params, cache_v[:, n, :], vs)
                    load(params, b_gate_col[:, :], of_layer("b_gate").rearrange("a (j p) -> p (a j)", p=P), True)
                    load(params, b_sp_col[:, :], of_layer("b_spatial").rearrange("a g p -> p (a g)"), True)

                    def split_hi(n):
                        m = SPLIT_UNITS[n]
                        r, full = raw_at(m)
                        act.wait_ge(raw_full[r], full)
                        if n >= RING:
                            wait_filled(act, LAST_USE[n - RING])
                        tally.did(act.activation(w_hi[:, n % RING, :, :], raw[:, r, :, :], ACT.Copy), hi_made)

                    pt_b_done = 0
                    for e in ORDER:
                        kind = e[0]
                        if kind == "split":
                            split_hi(e[1])
                        elif kind == "mod" and e[1] >= 8:
                            g = e[1] - 8
                            if g < 3:
                                wait_filled(act, e)
                                for half in range(2):
                                    load(modg_in, mod_raw[:, half, :, :],
                                         unit_source("mod", 0, half * UK, (9 + g) * COLS))
                        elif kind == "h":
                            wait_drained(act, e)
                            tally.did(act.activation(h_hi[:, e[1], :], hf[:, e[1] % 2, :], ACT.Copy), hh_ready)
                        elif kind == "in":
                            _, g, t = e
                            br = next((b for b in "ab" if g == KV_GROUP[b] or g in Q_GROUP[b] or g in G_GROUP[b]), "c")
                            if br == "a" and (g == KV_GROUP["a"] or g in Q_GROUP["a"]):
                                s = wait_filled(act, e)
                                n = SQ_NO[e]
                                if n >= 2:
                                    act.wait_ge(staged, SQ_STAGED[n - 2])
                                w = P if g == KV_GROUP["a"] else COLS
                                tally.did(act.activation(square[:, n % 2, 0:w], slot(s)[:, 0:w], ACT.Square), sq_ready)
                            elif br in "ab" and g in G_GROUP[br]:
                                s = wait_filled(act, e)
                                tally.did(act.activation(gate_br[:, t, :], slot(s)[:, 0:COLS], ACT.Silu), drained[s])
                            elif g in GC_GROUP:
                                s = wait_filled(act, e)
                                half = GC_GROUP.index(g) * COLS
                                tally.did(act.activation(ug[:, t, half:half + COLS], slot(s)[:, 0:COLS], ACT.Silu),
                                          drained[s])
                            elif g in V_GROUP:
                                s = wait_filled(act, e)
                                if g == V_GROUP[0] and t == 0:
                                    act.wait_ge(merged, 2 * KT_D - KT_D)
                                    load(late, sgu_g[:, :], of_layer("sgu_g").to_broadcast([P, BW]))
                                    load(late, sgu_b[:, :], of_layer("sgu_b").to_broadcast([P, BW]))
                                half = V_GROUP.index(g) * COLS
                                tally.did(act.activation(vn[:, t, half:half + COLS], slot(s)[:, 0:COLS], ACT.Copy),
                                          drained[s])
                        elif kind == "kt":
                            s = wait_filled(act, e)
                            _, br, t = e
                            tally.did(act.activation(k_hi[:, :, t * P:(t + 1) * P],
                                                     slot(s)[:, 0:2 * P].rearrange("p (v n) -> p v n", v=NKV), ACT.Copy),
                                      t_hi)
                            if t == CACHE:
                                act.wait_ge(staged, STAGED[("k", br, 0)])
                                load(state_out, outs[f"state_{br}_k"][0, bass.ds(layer, 1)].rearrange("a p h d -> p (a h) d"),
                                     k_st[:, 0, :, 0, :])
                                load(state_out, outs[f"state_{br}_v"][0, bass.ds(layer, 1)].rearrange("a p h d -> p (a h d)"),
                                     vals[:, 0, :])
                        elif kind == "qt":
                            s = wait_filled(act, e)
                            _, br, kv, t = e
                            scale = 1.0 if br == "a" else HD ** -0.5
                            tally.did(act.activation(q_t[0:HD, :, t * P:(t + 1) * P],
                                                     slot(s)[0:HD, 0:GRP * P].rearrange("p (h n) -> p h n", h=GRP),
                                                     ACT.Copy, scale=scale), t_hi)
                        elif kind == "s":
                            _, br, kv, i = e
                            t, hh = QUERY_TILES[i // GRP], i % GRP
                            n = len(key_slots(br, t)) * P
                            u = UNIT_NO[(br, kv, i)]
                            s = wait_filled(act, e)
                            act.wait_ge(nm_ready, u + 1)
                            if i >= 2:
                                act.wait_ge(p_turned, u - 1)
                            c = u % 8
                            tally.did(act.activation(prob[:, i % 2, 0:n], slot(s)[:, 0:n], ACT.Exp,
                                                     bias=neg_top[:, c:c + 1], accum_out=psums[:, c:c + 1]), drained[s])
                            if br == "b":
                                head = kv * GRP + hh
                                tally.did(act.activation(psink[:, c:c + 1], sink[:, head:head + 1], ACT.Exp,
                                                         bias=neg_top[:, c:c + 1]), sink_exp)
                        elif kind == "pt":
                            _, br, kv, i = e
                            nk = len(key_slots(br, QUERY_TILES[i // GRP]))
                            first = pt_split(nk)
                            if nk > first:
                                u = UNIT_NO[(br, kv, i)]
                                act.wait_ge(p_turned, u + 1)
                                if i >= 2:
                                    act.wait_ge(o_full, u - 1)
                                tally.did(act.activation(prob_t[:, i % 2, first:nk, :].rearrange("p k n -> p (k n)"),
                                                         ps[:, 5, 0:(nk - first) * P], ACT.Copy), pt_b)
                        elif kind == "ot":
                            _, br, kv, j = e
                            o = TILE_NO[(br, kv, j)]
                            t = QUERY_TILES[j]
                            act.wait_ge(ot_full, o + 1)
                            if kv == 0 and j == 0 and br == "b":
                                wait_filled(act, ("y", 0, KT_D - 1))
                            tally.did(act.activation(o_hi[:, 2 * kv:2 * kv + 2, t * P:(t + 1) * P],
                                                     ps[:, 6 + o % 2, 0:2 * P].rearrange("p (c n) -> p c n", c=2), ACT.Copy),
                                      t_hi)
                        elif kind == "z":
                            _, r, j = e
                            s = wait_filled(act, e)
                            n = r * KT_D + j
                            if n >= 2:
                                wait_drained(act, ("y", (n - 2) // KT_D, (n - 2) % KT_D))
                            tally.did(act.activation(sg[:, j % 2, :].rearrange("p (b n) -> p b n", b=2),
                                                     ps[:, 2 * s:2 * s + 2, 0:HALF], ACT.Sigmoid,
                                                     bias=b_gate_col[:, n:n + 1]), drained[s])
                            if r == 2 and j == 0:
                                for half in range(2):
                                    load(modg_in, mod_raw[:, half, :, :], unit_source("mod", 0, half * UK, 8 * COLS))
                                load(ends, b_modg_bc[:, :], of_layer("b_mod")[:, 2 * D:3 * D].to_broadcast([P, D]))
                                load(ends, ln_g_bc[:, :], of_layer("ln_g").to_broadcast([P, D]))
                                load(ends, ln_b_bc[:, :], of_layer("ln_b").to_broadcast([P, D]))
                        elif kind == "ct":
                            g = e[1]
                            s = wait_filled(act, e)
                            tally.did(act.activation(o_hi[:, g, :], slot(s)[:, 0:TOK], ACT.Copy), t_hi)
                        elif kind == "m":
                            j = e[1]
                            act.wait_ge(merged, 2 * KT_D + j + 1 - KT_D)
                            if j == 0:
                                wait_filled(act, ("z", 2, KT_D - 1))
                            tally.did(act.activation(h_hi[:, j, :], merge[:, j, :], ACT.Copy), m_hi)
                        elif kind == "out" and e[1] == D // COLS - 1:
                            if e[2] >= 1:
                                normalise(act, tally, e[2] - 1)
                    normalise(act, tally, T - 1)
                    act.wait_ge(state_out, 64)

                @block.vector
                def _(dve):
                    tally = Tally(dve, dve_step)
                    did = tally.did
                    rstds = [0]

                    def after(token):
                        dve.wait_ge(*token)

                    def ask_rstd(instruction):
                        return did(instruction, var_ready)

                    def await_rstd():
                        rstds[0] += 1
                        dve.wait_ge(rstd_ready, rstds[0])

                    def moments(t, halves):
                        for n, src in enumerate(halves):
                            tok = did(dve.bn_stats(bn[:, t, n, :], src))
                        after(tok)
                        return dve.bn_aggr(mv[:, t, :], bn[:, t, 0:len(halves), :])

                    def drain(instruction, stage):
                        did(instruction, drained[PLACE[stage][0]])
                        wait_drained(dve, stage)

                    def rotate(dst, src, c, tab, heads, dup, stage):
                        half = HD // 2
                        rc = rot_c[:, c, 0:heads * HD].rearrange("p (h d) -> p h d", h=heads)
                        rs = rot_s[:, c, 0:heads * HD].rearrange("p (h d) -> p h d", h=heads)
                        did(dve.tensor_tensor(rc, src, tab[:, 0:1, :].to_broadcast([P, heads, HD]), ALU.mult))
                        did(dve.tensor_tensor(rs[:, :, 0:half], src[:, :, half:HD],
                                              tab[:, 1:2, 0:half].to_broadcast([P, heads, half]), ALU.mult))
                        last = dve.tensor_tensor(rs[:, :, half:HD], src[:, :, 0:half],
                                                 tab[:, 1:2, half:HD].to_broadcast([P, heads, half]), ALU.mult)
                        if stage is None:
                            after(did(last))
                        else:
                            drain(last, stage)
                        if dup:
                            rc = rc.unsqueeze(2).to_broadcast([P, heads, 2, HD])
                            rs = rs.unsqueeze(2).to_broadcast([P, heads, 2, HD])
                        did(dve.tensor_tensor(dst, rc, rs, ALU.add), staged)

                    def queries_or_keys(e, br, is_key):
                        _, g, t = e
                        s = wait_filled(dve, e)
                        heads = NKV if is_key else GRP
                        src = slot(s)[:, 0:heads * HD].rearrange("p (h d) -> p h d", h=heads)
                        if br == "a":
                            dve.wait_ge(sq_ready, SQ_NO[e] + 1)
                        if is_key and br == "b" and t == 0:
                            dve.wait_ge(state_out, 32)
                            for j in (KT_D - 2, KT_D - 1):
                                wait_drained(dve, ("y", 0, j))
                        if is_key:
                            did(dve.tensor_copy(vals[:, t, :], slot(s)[:, P:2 * P]))
                            dst = k_st[:, k_buffer(t), :, :, :]
                        else:
                            dst = q_st[:, t % 2, :].rearrange("p (h d) -> p h d", h=heads)
                        if is_key and t >= 3:
                            wait_filled(dve, ("kt", br, t - 2))
                        if not is_key and t >= 2:
                            wait_filled(dve, ("qt", br, Q_GROUP[br].index(g), t - 2))
                        stage = e
                        turn = tally.count(staged)
                        if turn >= 2:
                            dve.wait_ge(staged, turn - 1)
                        if br == "a":
                            c = SQ_NO[e] % 2
                            ask_rstd(dve.tensor_reduce(ssq[:, c, 0:heads],
                                                       square[:, c, 0:heads * HD].rearrange("p (h d) -> p h d", h=heads),
                                                       axis=AX.X, op=ALU.add))
                            await_rstd()
                            flat = square[:, c, 0:heads * HD].rearrange("p (h d) -> p h d", h=heads)
                            drain(dve.tensor_tensor(flat, src, rqk[:, c, 0:heads].unsqueeze(2).to_broadcast([P, heads, HD]),
                                                    ALU.mult), e)
                            src, stage = flat, None
                        tab = 1 if is_key else 0
                        if t > 0:
                            w = table[:, tab, t - 1, :, :] if br == "a" else rope[:, t - 1, :, :]
                            rotate(dst, src, turn % 2, w, heads, is_key, stage)
                        elif br == "a":
                            w = norm[:, tab, 0:1, :]
                            if is_key:
                                did(dve.tensor_tensor(dst, src.unsqueeze(2).to_broadcast([P, heads, 2, HD]),
                                                      w.unsqueeze(2).to_broadcast([P, heads, 2, HD]), ALU.mult), staged)
                            else:
                                did(dve.tensor_tensor(dst, src, w.to_broadcast([P, heads, HD]), ALU.mult), staged)
                        else:
                            c = rot_c[:, turn % 2, 0:heads * HD].rearrange("p (h d) -> p h d", h=heads)
                            drain(dve.tensor_copy(c, src), e)
                            if is_key:
                                c = c.unsqueeze(2).to_broadcast([P, heads, 2, HD])
                            did(dve.tensor_copy(dst, c), staged)

                    for t in range(T):
                        tok = did(moments(t, [x[:, t, 0:512], x[:, t, 512:D]]))
                    after(tok)
                    ask_rstd(dve.tensor_copy(rstd[:, :], mv[:, :, 1]))
                    await_rstd()
                    for t in range(T):
                        did(dve.tensor_scalar(xn[:, t, :], x[:, t, :], mv[:, t, 0:1], rstd[:, t:t + 1],
                                              ALU.subtract, ALU.mult), xn_ready)
                    dve.wait_ge(params, 16 * PARAM_LOADS)
                    after(did(dve.tensor_scalar(norm[:, 1, :, :], norm[:, 1, :, :], float(HD) ** 0.5, None, ALU.mult)))
                    for n in range(2):
                        did(dve.tensor_tensor(table[:, n, :, :, :].rearrange("p t c d -> p t (c d)"),
                                              rope[:, :, :, :].rearrange("p t c d -> p t (c d)"),
                                              norm[:, n, :, :].rearrange("p c d -> p (c d)").unsqueeze(1)
                                              .to_broadcast([P, T - 1, 2 * HD]), ALU.mult))

                    for e in ORDER:
                        kind = e[0]
                        if kind == "mod":
                            s = wait_filled(dve, e)
                            if e[1] < 8:
                                did(dve.tensor_copy(mod_rows[:, e[1] * COLS:(e[1] + 1) * COLS], slot(s)[:, 0:COLS]),
                                    drained[s])
                            else:
                                g = e[1] - 8
                                did(dve.tensor_copy(gate_rows[:, g % 2, :], slot(s)[:, 0:COLS]), drained[s])
                                s = wait_filled(dve, ("bc", e[1]))
                                if g == 0:
                                    dve.wait_ge(ends, 48)
                                cols = slice(g * COLS, (g + 1) * COLS)
                                did(dve.tensor_tensor(gate_bc[:, :, cols], ps[:, 2 * s:2 * s + 2, 0:COLS],
                                                      b_modg_bc[:, cols].unsqueeze(1).to_broadcast([P, 2, COLS]), ALU.add),
                                    drained[s])
                        elif kind == "cols":
                            s = wait_filled(dve, e)
                            cols = slot(s)[:, 0:4 * KT_D].rearrange("p (j v) -> p j v", v=2)
                            bias = b_mod_col[:, :].unsqueeze(2).to_broadcast([P, 2 * KT_D, 2])
                            after(did(dve.tensor_tensor(ada[:, :, :], cols, bias, ALU.add)))
                            did(dve.tensor_scalar(ada[:, KT_D:, :], ada[:, KT_D:, :], 1.0, None, ALU.add))
                            drain(dve.tensor_copy(w_sp_t[:, :, :].rearrange("p g n -> p (g n)"), ps[:, 2 * s + 1, :]), e)
                        elif kind == "h":
                            j = e[1]
                            s = wait_filled(dve, e)
                            if j >= 2:
                                dve.wait_ge(h_ready, j - 1)
                            did(dve.tensor_scalar(hf[:, j % 2, 0:P], slot(s)[:, 0:P], ada[:, KT_D + j, 0:1],
                                                        ada[:, j, 0:1], ALU.mult, ALU.add))
                            did(dve.tensor_scalar(hf[:, j % 2, P:TOK], slot(s)[:, P:TOK], ada[:, KT_D + j, 1:2],
                                                  ada[:, j, 1:2], ALU.mult, ALU.add), drained[s])
                            dve.wait_ge(hh_ready, j + 1)
                            did(dve.tensor_tensor(h_lo[:, j, :], hf[:, j % 2, :], h_hi[:, j, :], ALU.subtract), h_ready)
                        elif kind == "in":
                            _, g, t = e
                            for br in "ab":
                                if g == KV_GROUP[br]:
                                    queries_or_keys(e, br, True)
                                elif g in Q_GROUP[br]:
                                    queries_or_keys(e, br, False)
                            if g in V_GROUP:
                                n = V_GROUP.index(g)
                                wait_drained(dve, e)
                                did(dve.bn_stats(bn[:, t, n, :], vn[:, t, n * COLS:(n + 1) * COLS]))
                                if n == 1:
                                    after((dve_step, tally.count(dve_step)))
                                    tok = did(dve.bn_aggr(mv[:, t, :], bn[:, t, :, :]))
                                if n == 1 and t == T - 1:
                                    after(tok)
                                    ask_rstd(dve.tensor_copy(rstd[:, :], mv[:, :, 1]))
                                    await_rstd()
                                    dve.wait_ge(late, 32)
                                    for q in range(T):
                                        tok = did(dve.tensor_scalar(vn[:, q, :], vn[:, q, :], mv[:, q, 0:1],
                                                                    rstd[:, q:q + 1], ALU.subtract, ALU.mult))
                                        after(tok)
                                        tok = did(dve.tensor_tensor(vn[:, q, :], vn[:, q, :], sgu_g[:, :], ALU.mult))
                                        after(tok)
                                        did(dve.tensor_tensor(vn[:, q, :], vn[:, q, :], sgu_b[:, :], ALU.add), vn_ready)
                            elif g in U_GROUP:
                                s = wait_filled(dve, e)
                                half = U_GROUP.index(g) * COLS
                                wait_drained(dve, ("in", GC_GROUP[U_GROUP.index(g)], t))
                                did(dve.tensor_tensor(ug[:, t, half:half + COLS], slot(s)[:, 0:COLS],
                                                      ug[:, t, half:half + COLS], ALU.mult), drained[s])
                        elif kind == "kt":
                            _, br, t = e
                            s = wait_filled(dve, e)
                            dve.wait_ge(t_hi, T_HI_NO[e])
                            did(dve.tensor_tensor(k_lo[:, :, t * P:(t + 1) * P],
                                                  slot(s)[:, 0:2 * P].rearrange("p (v n) -> p v n", v=NKV),
                                                  k_hi[:, :, t * P:(t + 1) * P], ALU.subtract), drained[s])
                        elif kind == "qt":
                            _, br, kv, t = e
                            s = wait_filled(dve, e)
                            dve.wait_ge(t_hi, T_HI_NO[e])
                            scale = 1.0 if br == "a" else HD ** -0.5
                            did(dve.scalar_tensor_tensor(q_t[HD:P, :, t * P:(t + 1) * P],
                                                         slot(s)[0:HD, 0:GRP * P].rearrange("p (h n) -> p h n", h=GRP),
                                                         scale, q_t[0:HD, :, t * P:(t + 1) * P], ALU.mult, ALU.subtract),
                                drained[s])
                        elif kind == "s":
                            _, br, kv, i = e
                            t, hh = QUERY_TILES[i // GRP], i % GRP
                            n = len(key_slots(br, t)) * P
                            u = UNIT_NO[(br, kv, i)]
                            c = u % 8
                            s = wait_filled(dve, e)
                            after(did(dve.tensor_reduce(top[:, c:c + 1], slot(s)[:, 0:n], axis=AX.X, op=ALU.max)))
                            if br == "a":
                                did(dve.tensor_scalar(neg_top[:, c:c + 1], top[:, c:c + 1], -1.0, None, ALU.mult), nm_ready)
                            else:
                                head = kv * GRP + hh
                                did(dve.tensor_scalar(neg_top[:, c:c + 1], top[:, c:c + 1], sink[:, head:head + 1], -1.0,
                                                      ALU.max, ALU.mult), nm_ready)
                        elif kind == "pt":
                            _, br, kv, i = e
                            nk = len(key_slots(br, QUERY_TILES[i // GRP]))
                            first = min(pt_split(nk), nk)
                            u = UNIT_NO[(br, kv, i)]
                            dve.wait_ge(p_turned, u + 1)
                            if i >= 2:
                                dve.wait_ge(o_full, u - 1)
                            did(dve.tensor_copy(prob_t[:, i % 2, 0:first, :].rearrange("p k n -> p (k n)"),
                                                ps[:, 4, 0:first * P]), pt_a)
                        elif kind == "pv" and e[3] % GRP == GRP - 1:
                            _, br, kv, i = e
                            u = UNIT_NO[(br, kv, i)]
                            o = TILE_NO[(br, kv, i // GRP)]
                            t = QUERY_TILES[i // GRP]
                            c0 = (u - 3) % 8
                            den = psums[:, c0:c0 + GRP]
                            ro = rinv[:, o % 2, :]
                            wait_drained(dve, ("s", br, kv, i))
                            if br == "b":
                                dve.wait_ge(sink_exp, u + 1 - SINK_FIRST)
                                after(did(dve.tensor_tensor(den, den, psink[:, c0:c0 + GRP], ALU.add)))
                            after(did(dve.reciprocal(ro, den)))
                            if o >= 2:
                                dve.wait_ge(ot_full, o - 1)
                            dve.wait_ge(o_full, u + 1)
                            dst = og[:, o % 2, :].rearrange("p (h d) -> p h d", h=GRP)
                            after(did(dve.tensor_tensor(dst, ps[:, 6 + o % 2, 0:COLS].rearrange("p (h d) -> p h d", h=GRP),
                                                        ro.unsqueeze(2).to_broadcast([P, GRP, HD]), ALU.mult)))
                            did(dve.tensor_tensor(og[:, o % 2, :], og[:, o % 2, :], gate_br[:, t, :], ALU.mult), og_ready)
                        elif kind == "ot":
                            _, br, kv, j = e
                            o = TILE_NO[(br, kv, j)]
                            t = QUERY_TILES[j]
                            dve.wait_ge(t_hi, T_HI_NO[e])
                            dst = slice(2 * kv, 2 * kv + 2), slice(t * P, (t + 1) * P)
                            did(dve.tensor_tensor(o_lo[:, dst[0], dst[1]],
                                                  ps[:, 6 + o % 2, 0:2 * P].rearrange("p (c n) -> p c n", c=2),
                                                  o_hi[:, dst[0], dst[1]], ALU.subtract), ot_done)
                        elif kind == "y":
                            _, r, j = e
                            s = wait_filled(dve, e)
                            wait_drained(dve, ("z", r, j))
                            y = ps[:, 2 * s:2 * s + 2, 0:HALF]
                            g2 = sg[:, j % 2, :].rearrange("p (b n) -> p b n", b=2)
                            if r == 0:
                                did(dve.tensor_tensor(merge[:, j, :].rearrange("p (b n) -> p b n", b=2), y, g2, ALU.mult),
                                    drained[s])
                            else:
                                n = (r - 1) * KT_D + j
                                if n >= 2:
                                    dve.wait_ge(merged, n - 1)
                                did(dve.tensor_tensor(gy[:, j % 2, :].rearrange("p (b n) -> p b n", b=2), y, g2, ALU.mult),
                                    drained[s])
                        elif kind == "mix":
                            g = e[1]
                            s = wait_filled(dve, e)
                            if g == 0:
                                for h in range(2):
                                    for t in range(T):
                                        wait_drained(dve, ("in", U_GROUP[h], t))
                            did(dve.scalar_tensor_tensor(ug[:, :, g * P:(g + 1) * P],
                                                         slot(s)[:, 0:TOK].rearrange("p (t n) -> p t n", t=T),
                                                         b_sp_col[:, g:g + 1], ug[:, :, g * P:(g + 1) * P],
                                                         ALU.add, ALU.mult), drained[s])
                        elif kind == "ct":
                            g = e[1]
                            s = wait_filled(dve, e)
                            dve.wait_ge(t_hi, T_HI_NO[e])
                            did(dve.tensor_tensor(o_lo[:, g, :], slot(s)[:, 0:TOK], o_hi[:, g, :], ALU.subtract), drained[s])
                        elif kind == "m":
                            j = e[1]
                            dve.wait_ge(m_hi, j + 1)
                            did(dve.tensor_tensor(h_lo[:, j, :], merge[:, j, :], h_hi[:, j, :], ALU.subtract), m_ready)
                        elif kind == "out":
                            _, g, t = e
                            s = wait_filled(dve, e)
                            n = g * T + t
                            cols = slice(g * COLS, (g + 1) * COLS)
                            drain(dve.tensor_tensor(scaled[:, n % 2, :], slot(s)[:, 0:COLS],
                                                    gate_bc[:, min(t, 1), cols], ALU.mult), e)
                            tok = did(dve.scalar_tensor_tensor(x[:, t, cols], x[:, t, cols], ALPHA, scaled[:, n % 2, :],
                                                               ALU.mult, ALU.add))
                            if g == D // COLS - 1:
                                after(tok)
                                tok = ask_rstd(moments(t, [x[:, t, 0:512], x[:, t, 512:D]]))
                                after(tok)
                                await_rstd()
                                did(dve.scalar_tensor_tensor(nmr[:, t:t + 1], mv[:, t, 0:1], -1.0, rstd[:, t:t + 1],
                                                             ALU.mult, ALU.mult), nmr_ready)
                                if t >= 1:
                                    apply_ln_g(dve, did, t - 1)
                    apply_ln_g(dve, did, T - 1)

                @block.gpsimd
                def _(pool):
                    tally = Tally(pool, pool_step)
                    did = tally.did
                    asked = [0]

                    def root(out, src, eps):
                        asked[0] += 1
                        pool.wait_ge(var_ready, asked[0])
                        n = out.shape[-1]
                        pool.wait_ge(*did(pool.tensor_scalar(with_eps[:, 0:n], src, eps, None, ALU.add)))
                        did(pool.tensor_tensor(out, with_eps[:, 0:n], minus_half[:, 0:n], ALU.pow), rstd_ready)

                    root(rstd[:, :], rstd[:, :], EPS)
                    for e in ORDER:
                        kind = e[0]
                        if kind == "split":
                            n = e[1]
                            r, _ = raw_at(SPLIT_UNITS[n])
                            pool.wait_ge(hi_made, n + 1)
                            did(pool.tensor_tensor(w_lo[:, n % RING, :, :].rearrange("p k n -> p (k n)"),
                                                   raw[:, r, :, :].rearrange("p k n -> p (k n)"),
                                                   w_hi[:, n % RING, :, :].rearrange("p k n -> p (k n)"),
                                                   ALU.subtract), w_ready)
                        elif kind == "in" and e in SQ_NO:
                            heads = NKV if e[1] == KV_GROUP["a"] else GRP
                            c = SQ_NO[e] % 2
                            root(rqk[:, c, 0:heads], ssq[:, c, 0:heads], HD * EPS)
                        elif kind == "in" and e[1] == V_GROUP[1] and e[2] == T - 1:
                            root(rstd[:, :], rstd[:, :], EPS)
                        elif kind == "y" and e[1] >= 1:
                            _, r, j = e
                            wait_drained(pool, e)
                            did(pool.tensor_tensor(merge[:, j, :], merge[:, j, :], gy[:, j % 2, :], ALU.add), merged)
                        elif kind == "out" and e[1] == D // COLS - 1:
                            t = e[2]
                            root(rstd[:, t:t + 1], mv[:, t, 1:2], EPS)
                            if t >= 1:
                                add_ln_b(pool, did, t - 1)
                    add_ln_b(pool, did, T - 1)

        with nc.Block() as block:
            @block.sync
            def _(sp):
                sp.dma_start(outs["y_prompt"][0], x[:, 0, :]).then_inc(final, 16)
                for t in range(1, T):
                    sp.dma_start(outs["y_sample"][0, (t - 1) * P:t * P, :], x[:, t, :]).then_inc(final, 16)
                sp.wait_ge(final, 16 * T)


def k_buffer(t):
    return 0 if t == 0 else 1 + (t - 1) % 2


def pt_split(n):
    return {1: 1, 3: 2, 4: 2, 5: 3}[n]


def key_runs(keys):
    runs = []
    for n, (s, _) in enumerate(keys):
        if runs and runs[-1][2] + runs[-1][1] == s * P and runs[-1][1] < 512:
            runs[-1][1] += P
        else:
            runs.append([n * P, P, s * P])
    return runs


def slot_uses_before(stage, s):
    n = 0
    for e in ORDER:
        if e == stage:
            break
        n += e in PLACE and PLACE[e][0] == s
        if e[0] == "mod" and e[1] >= 8:
            n += PLACE[("bc", e[1])][0] == s
    return n


def numbers():
    staged, sq, sq_staged, t_hi, unit, tile, pt = {}, {}, [], {}, {}, {}, {}
    n_staged = n_hi = n_a = n_b = 0
    for e in ORDER:
        if e[0] == "in":
            _, g, t = e
            for br in "ab":
                if g == KV_GROUP[br] or g in Q_GROUP[br]:
                    n_staged += 1
                    key = ("k", br, t) if g == KV_GROUP[br] else ("q", br, Q_GROUP[br].index(g), t)
                    staged[key] = n_staged
                    if br == "a":
                        sq[e] = len(sq)
                        sq_staged.append(n_staged)
        elif e[0] in ("kt", "qt", "ct", "ot"):
            n_hi += 1
            t_hi[e] = n_hi
        elif e[0] == "s":
            unit[e[1:]] = len(unit)
            if e[3] % GRP == 0:
                tile[(e[1], e[2], e[3] // GRP)] = len(tile)
        elif e[0] == "pt":
            pt[e[1:]] = (n_a, n_b)
            nk = len(key_slots(e[1], QUERY_TILES[e[3] // GRP]))
            n_a += 1
            n_b += nk > pt_split(nk)
    return staged, sq, sq_staged, t_hi, unit, tile, pt


STAGED, SQ_NO, SQ_STAGED, T_HI_NO, UNIT_NO, TILE_NO, PT_COUNT = numbers()
SINK_FIRST = UNIT_NO[("b", 0, 0)]
PARAM_LOADS = 1 + 6 + 1 + 6 + 2

_INS = ['x_prompt', 'x_sample', 'cache_a_k', 'cache_a_v', 'cache_b_k', 'cache_b_v', 'c', 'c_ctx', 'w_mod', 'b_mod',
        'w_in', 'q_norm', 'k_norm', 'sink', 'sgu_g', 'sgu_b', 'w_spatial', 'b_spatial', 'w_proj_a', 'w_proj_b',
        'w_proj_c', 'w_gate', 'b_gate', 'w_out', 'ln_g', 'ln_b']
_OUTS = {"y_prompt": (1, P, D), "y_sample": (1, 4 * P, D), "state_a_k": (1, DEPTH, P, NKV, HD),
         "state_a_v": (1, DEPTH, P, NKV, HD), "state_b_k": (1, DEPTH, P, NKV, HD), "state_b_v": (1, DEPTH, P, NKV, HD)}


def rope_constants():
    grid_w, freqs, n = 64, HD // 4, 4 * P
    row = np.repeat(np.arange(n // grid_w, dtype=np.float32), grid_w)
    col = np.tile(np.arange(grid_w, dtype=np.float32), n // grid_w)
    inv = np.power(np.float32(10000.0), -np.arange(freqs, dtype=np.float32) / np.float32(freqs))
    ang = np.concatenate([row[:, None] * inv, col[:, None] * inv], axis=-1)
    c, s = np.cos(ang), np.sin(ang)
    both = np.stack([np.concatenate([c, c], -1), np.concatenate([-s, s], -1)], axis=1)
    return np.ascontiguousarray(both.reshape(4, P, 2, HD).transpose(1, 0, 2, 3)).astype(np.float32)


def kernel(**inputs):
    import concourse.bacc as _bacc
    from concourse.bass_utils import run_bass_kernel_spmd as _run

    nc = _bacc.Bacc("TRN2", target_bir_lowering=False, num_devices=1,
                     dynamic_dma_scratch_size=1024)
    arrays, args, outs = {}, {}, {}
    for name in _INS:
        v = np.ascontiguousarray(inputs[name])
        arrays[f"in_{name}"] = v
        args[name] = nc.dram_tensor(f"in_{name}", v.shape, mybir.dt.from_np(v.dtype), kind="ExternalInput").ap()
    arrays["rope_table"] = rope_constants()
    args["rope"] = nc.dram_tensor("rope_table", (P, T - 1, 2, HD), F32, kind="ExternalInput").ap()
    for name, shape in _OUTS.items():
        outs[name] = nc.dram_tensor(name, shape, F32, kind="ExternalOutput").ap()
    build(nc, args, outs)
    r = _run(nc, [arrays], core_ids=[0])
    return tuple(r.results[0][name] for name in _OUTS)
```

```python
from contextlib import ExitStack

import numpy as np

import concourse.bass as bass
from concourse import mybir

P = 128
F32 = mybir.dt.float32
F32R = mybir.dt.float32r
ALU = mybir.AluOpType
ACT = mybir.ActivationFunctionType
AX = mybir.AxisListType

D = 1024
DEPTH = 2
T = 5
TOK = T * P
HALF = TOK // 2
HD = 64
NKV = 2
GRP = 4
KT_D = D // P
BW = 512
KT_B = BW // P
COLS = 256
UK = 4
RAW = 3
RING = 4
EPS = 1e-6
ALPHA = (2 * DEPTH) ** 0.25
NEG = -1e30
CACHE = T

UNIT = 1024
BANKS = 8

IN_GROUPS = {"q_a": (0, 512), "kv_a": (512, 256), "g_a": (768, 512),
             "q_b": (1280, 512), "kv_b": (1792, 256), "g_b": (2048, 512),
             "u_c": (2560, 512), "v_c": (3072, 512), "g_c": (3584, 512)}
QUERY_TILES = (1, 2, 3, 4, 0)
HEADS = NKV * GRP


def key_slots(branch, tile):
    if tile == 0:
        return [(0, None)]
    if branch == "a":
        return [(s, None) for s in (1, 2, 3, 4, CACHE)]
    band = [(s, {-1: "before", 0: None, 1: "after"}[s - tile]) for s in (tile - 1, tile, tile + 1) if 1 <= s < T]
    return band + [(CACHE, None)]


def layer_order():
    order, units, split_units, uses, last_use = [], [], [], {}, {}
    waiting, turned = [], []

    def use(kind, index, rows, col, width):
        mine = []
        nk = UNIT // width
        for k0 in range(0, rows, nk):
            units.append((kind, index, k0, nk, col, width))
            mine.append(len(split_units))
            split_units.append(len(units) - 1)
        return mine

    def evacuate(n):
        for _ in range(min(n, len(waiting))):
            name, t = waiting.pop(0)
            order.append(("in", name, t))
            turned.append((name, t))

    def turn(n):
        for _ in range(min(n, len(turned))):
            name, t = turned.pop(0)
            br = name[-1]
            if name.startswith("kv"):
                order.append(("kt", br, t))
                if t == T - 1:
                    order.append(("kt", br, CACHE))
            if name.startswith("q"):
                order.extend([("qt", br, kv, t) for kv in range(NKV)])

    def dense(name, heavy):
        col, width = IN_GROUPS[name]
        mine = use("in", 0, KT_D, col, width)
        uses[name] = mine
        for n, u in enumerate(mine):
            evacuate(3 if n == 0 else 1)
            order.append(("mm", name, n))
            last_use[u] = ("mm", name, n) if u != mine[-1] else ("in", name, 1)
            turn((2, 1, 2, 0)[n])
        waiting.extend((name, t) for t in range(T))
        if not heavy:
            turn(T)
            evacuate(T)
            turned.clear()

    def flush():
        while waiting or turned:
            evacuate(1)
            turn(1)

    def attention(br):
        n = HEADS * T
        order.extend([("s", br, 0), ("s", br, 1)])
        for i in range(n + 3):
            if i < n:
                order.append(("pt", br, i))
            if i + 2 < n:
                order.append(("s", br, i + 2))
            if 1 <= i <= n:
                order.append(("pv", br, i - 1))
            if i >= GRP + 1 and (i - 2) % GRP == GRP - 1:
                order.append(("ot", br, (i - 2) // GRP))

    def gates(r):
        for g in range(D // COLS):
            gate = use("gate", 0, KT_D, r * D + g * COLS, COLS)
            proj = use("proj", r, KT_B, g * COLS, COLS)
            for j in (2 * g, 2 * g + 1):
                uses[("z", r, j)] = gate
                uses[("y", r, j)] = proj
            if (r, g) == (2, D // COLS - 1):
                order.extend([("z", r, 2 * g), ("bc", 7 + g), ("z", r, 2 * g + 1)])
                order.extend([("m", j) for j in range(2 * g)])
                order.extend([("y", r, 2 * g), ("y", r, 2 * g + 1)])
            else:
                order.append(("z", r, 2 * g))
                if r == 2 and g:
                    order.append(("bc", 7 + g))
                order.extend([("y", r, 2 * g), ("z", r, 2 * g + 1), ("y", r, 2 * g + 1)])
            for u in gate:
                last_use[u] = ("z", r, 2 * g + 1)
            for u in proj:
                last_use[u] = ("y", r, 2 * g + 1)
            if r == 2:
                order.append(("mod", 8 + g))

    for b in range(8):
        units.extend([("mod", 0, 0, UK, b * COLS, COLS), ("mod", 0, UK, UK, b * COLS, COLS)])
        order.append(("mod", b))
    order.append(("cols",))
    order.extend([("h", j) for j in range(KT_D)])
    for r, br in enumerate("ab"):
        dense("kv_" + br, True)
        dense("q_" + br, True)
        dense("g_" + br, False)
        flush()
        attention(br)
        gates(r)
    for name in ("v_c", "g_c", "u_c"):
        dense(name, False)
    flush()
    for g in range(KT_B):
        order.append(("mix", g))
        if g:
            order.append(("ct", g - 1))
    order.append(("ct", KT_B - 1))
    gates(2)
    order.extend([("m", j) for j in range(KT_D - 2, KT_D)] + [("bc", 11)])
    uses["out0"] = use("out", 0, KT_D, 0, 512)
    uses["out1"] = use("out", 0, KT_D, 512, 512)
    for n, u in enumerate(uses["out0"]):
        order.append(("mm", "out0", n))
        last_use[u] = ("mm", "out0", n) if u != uses["out0"][-1] else ("out", 0, 1)
    order.extend([("out", 0, t) for t in range(T)] + [("out", 1, t) for t in range(T)])

    after = {}
    for n in range(RING, len(split_units)):
        after.setdefault(last_use[n - RING], []).append(n)
    for n, e in enumerate([("cols",), ("cols",), ("h", 3), ("h", 5), ("h", 7)][:RING]):
        after.setdefault(e, []).append(n)
    full = []
    for e in order:
        full.append(e)
        full.extend(("split", n) for n in after.get(e, []))
    return full, units, split_units, uses, last_use


ORDER, UNITS, SPLIT_UNITS, USES, LAST_USE = layer_order()


def bank_plan():
    place, former, count, holder = {}, {}, [0] * BANKS, [None] * BANKS
    taken, busy, clock = [-1] * BANKS, {}, 0

    def take(stage, banks, first=None, hold=False):
        nonlocal clock
        clock += 1
        if first is None:
            options = [b for b in range(0, BANKS, banks) if not any(b + i in busy.values() for i in range(banks))]
            first = min(options, key=lambda b: max(taken[b:b + banks]))
        if hold:
            busy[stage] = first
        place[stage] = (first, count[first])
        count[first] += 1
        former[stage] = sorted({holder[b] for b in range(first, first + banks)} - {None}, key=str)
        for b in range(first, first + banks):
            holder[b] = stage
            taken[b] = clock

    for e in ORDER:
        kind = e[0]
        if e in busy:
            clock += 1
            taken[busy.pop(e)] = clock
        if kind in ("mod", "bc", "kt", "qt"):
            take(e, 1)
        elif kind in ("cols", "h", "z", "y", "mix", "ct"):
            take(e, 2)
        elif kind == "mm" and e[2] == 0:
            for t in range(T):
                take(("out", 0, t) if e[1] == "out0" else ("in", e[1], t), 1, hold=True)
        elif kind == "out" and e[1] == 1:
            take(e, 1)
        elif kind == "s":
            take(e, 2, 2 * (e[2] % 2))
        elif kind == "ot":
            holder[6 + e[2] % 2] = e
    return place, former


PLACE, FORMER = bank_plan()


def build(nc, a, outs):
    with ExitStack() as ctx:
        def sb(name, shape, dt=F32):
            return ctx.enter_context(nc.sbuf_tensor(name, shape, dt))

        def sem(name):
            return ctx.enter_context(nc.semaphore(name))

        x = sb("x", [P, T, D])
        h_hi, h_lo = sb("h_hi", [P, KT_D, TOK], F32R), sb("h_lo", [P, KT_D, TOK], F32R)
        o_hi, o_lo = sb("o_hi", [P, KT_B, TOK], F32R), sb("o_lo", [P, KT_B, TOK], F32R)
        w_hi, w_lo = sb("w_hi", [P, RING, UNIT], F32R), sb("w_lo", [P, RING, UNIT], F32R)
        raw = sb("raw", [P, RAW, UNIT])
        ident = sb("ident", [P, P])
        ident_r = sb("ident_r", [P, P], F32R)
        mask_r = sb("mask_r", [P, 2, P], F32R)
        pick = sb("pick", [P, 2, P])
        silu_c = sb("silu_c", [P, KT_D, 32])
        c_in = sb("c_in", [P, 2, KT_D])
        rope = sb("rope", [P, T - 1, 2, HD])
        norm = sb("norm", [P, 2, 2, HD])
        table = sb("table", [P, 2, T - 1, 2, HD])
        sink = sb("sink", [P, 2 * GRP])
        b_mod_col = sb("b_mod_col", [P, 2 * KT_D])
        b_gate_col = sb("b_gate_col", [P, 3 * KT_D])
        b_sp_col = sb("b_sp_col", [P, KT_B])
        w_sp_t = sb("w_sp_t", [P, KT_B, P])
        cache_k = sb("cache_k", [P, 2, NKV, 2, HD])
        k_st = sb("k_st", [P, 3, NKV, 2, HD])
        cache_v = sb("cache_v", [P, 2, P])
        ada = sb("ada", [P, 2 * KT_D, 2])
        bn = sb("bn", [P, T, 2, 6])
        mv = sb("mv", [P, T, 2])
        rstd = sb("rstd", [P, T])
        nmr = sb("nmr", [P, T])
        with_eps = sb("with_eps", [P, 8])
        minus_half = sb("minus_half", [P, 8])
        ssq = sb("ssq", [P, 2, HEADS])
        rqk = sb("rqk", [P, 2, HEADS])
        top = sb("top", [P, 2 * GRP])
        neg_top = sb("neg_top", [P, 2 * GRP])
        psums = sb("psums", [P, 2 * GRP])
        psink = sb("psink", [P, 2 * GRP])
        rinv = sb("rinv", [P, 2, GRP])

        at0 = (nc.sbuf_base + 63) // 64 * 64
        MERGE = 20480
        ARENA = 59904
        sb("phase_memory", [P, (MERGE + ARENA + 64) // 4])

        def at(name, offset, shape, dt=F32):
            size = int(np.prod(shape[1:])) * 4
            assert offset + size <= MERGE + ARENA, name
            return nc.alloc_sbuf_tensor_at(name, shape, dt, offset=at0 + offset)

        merge = at("merge", 0, [P, KT_D, TOK])
        xn = at("xn", 0, [P, T, D])
        A0 = MERGE
        mod_rows = at("mod_rows", A0, [P, 2 * D])
        hf = at("hf", A0 + 10240, [P, 2, TOK])
        wsp_in = at("wsp_in", A0 + 16384, [P, KT_B, P])
        q_t = at("q_t", A0, [P, HEADS, TOK], F32R)
        k_hi = at("k_hi", A0 + 20480, [P, NKV, TOK + P], F32R)
        k_lo = at("k_lo", A0 + 26624, [P, NKV, TOK + P], F32R)
        vals = at("vals", A0 + 32768, [P, T, P])
        gate_br = at("gate_br", A0 + 35328, [P, T, BW])
        square = at("square", A0 + 45568, [P, 2, BW])
        rot_c = at("rot_c", A0 + 49664, [P, BW])
        rot_s = at("rot_s", A0 + 51712, [P, BW])
        q_st = at("q_st", A0 + 53760, [P, 3, BW])
        prob = at("prob", A0 + 45568, [P, 2, 5 * P])
        prob_t = at("prob_t", A0 + 50688, [P, 2, 5, P])
        og = at("og", A0 + 55808, [P, 2, COLS])
        vn = at("vn", A0, [P, T, BW])
        ug = at("ug", A0 + 10240, [P, T, BW])
        sgu_g = at("sgu_g", A0 + 20480, [P, BW])
        sgu_b = at("sgu_b", A0 + 22528, [P, BW])
        sg = at("sg", A0 + 45568, [P, 2, TOK])
        gy = at("gy", A0 + 50688, [P, 2, TOK])
        mod_raw = at("mod_raw", A0, [P, 2, UK, COLS])
        gate_bc = at("gate_bc", A0 + 8192, [P, 2, D])
        ln_g_bc = at("ln_g_bc", A0 + 16384, [P, D])
        ln_b_bc = at("ln_b_bc", A0 + 20480, [P, D])
        gate_rows = at("gate_rows", A0 + 24576, [P, 2, COLS])
        b_modg_bc = at("b_modg_bc", A0 + 26624, [P, D])
        scaled = at("scaled", A0 + 30720, [P, 2, BW])

        ps = ctx.enter_context(nc.psum_tensor("ps", [P, BANKS, 512], F32))

        def slot(b, banks=2):
            return ps[:, b:b + banks, :].rearrange("p b n -> p (b n)")

        loaded = sem("loaded")
        consts = sem("consts")
        setup = sem("setup")
        params = sem("params")
        late = sem("late")
        ends = sem("ends")
        raw_full = [sem(f"raw_full{i}") for i in range(RAW)]
        mod_half = sem("mod_half")
        modg_in = sem("modg_in")
        hi_made = sem("hi_made")
        w_ready = sem("w_ready")
        filled = [sem(f"filled{i}") for i in range(BANKS)]
        drained = [sem(f"drained{i}") for i in range(BANKS)]
        w_used = sem("w_used")
        var_ready, rstd_ready = sem("var_ready"), sem("rstd_ready")
        xn_ready, hh_ready, h_ready = sem("xn_ready"), sem("hh_ready"), sem("h_ready")
        wsp_ready = sem("wsp_ready")
        sq_ready, staged = sem("sq_ready"), sem("staged")
        t_hi = sem("t_hi")
        nm_ready = sem("nm_ready")
        sink_exp = sem("sink_exp")
        p_turned = sem("p_turned")
        pt_a, pt_b = sem("pt_a"), sem("pt_b")
        o_full, o_used = sem("o_full"), sem("o_used")
        og_ready, ot_full, ot_done = sem("og_ready"), sem("ot_full"), sem("ot_done")
        vn_ready = sem("vn_ready")
        merged = sem("merged")
        m_hi, m_ready = sem("m_hi"), sem("m_ready")
        nmr_ready, x_normed, x_scaled, x_done = (sem(n) for n in ("nmr_ready", "x_normed", "x_scaled", "x_done"))
        state_out = sem("state_out")
        pe_step, act_step, dve_step, pool_step = (sem(n) for n in ("pe_step", "act_step", "dve_step", "pool_step"))
        final = sem("final")
        per_layer = [w_used, params, late, ends, *raw_full, mod_half, modg_in, hi_made, w_ready, *filled, *drained, var_ready,
                     rstd_ready, xn_ready, hh_ready, h_ready, wsp_ready, sq_ready, staged, t_hi, nm_ready,
                     sink_exp, p_turned, pt_a, pt_b, o_full, o_used, og_ready, ot_full, ot_done, vn_ready,
                     merged, m_hi, m_ready, nmr_ready, x_normed, x_scaled,
                     x_done, state_out, pe_step, act_step, dve_step, pool_step]

        class Tally:

            def __init__(self, eng, step):
                self.eng, self.step, self.n = eng, step, {}

            def did(self, instruction, semaphore=None):
                s = semaphore or self.step
                instruction.then_inc(s, 1)
                self.n[s.name] = self.n.get(s.name, 0) + 1
                return s, self.n[s.name]

            def count(self, semaphore):
                return self.n.get(semaphore.name, 0)

        def wait_filled(eng, stage):
            s, k = PLACE[stage]
            eng.wait_ge(filled[s], k + 1)
            return s

        def wait_drained(eng, stage):
            s, k = PLACE[stage]
            eng.wait_ge(drained[s], k + 1)

        def raw_at(n):
            return n % RAW, 16 * (n // RAW + 1)

        with nc.Block() as block:
            @block.sync
            def _(sp):
                sp.dma_start(x[:, 0, :], a["x_prompt"][0]).then_inc(loaded, 16)
                for t in range(1, T):
                    sp.dma_start(x[:, t, :], a["x_sample"][0, (t - 1) * P:t * P, :]).then_inc(loaded, 16)

            @block.scalar
            def _(act):
                act.dma_start(c_in[:, 0, :], a["c_ctx"].rearrange("(j p) -> p j", p=P), allow_slow_non_contiguous=True).then_inc(setup, 16)
                act.dma_start(c_in[:, 1, :], a["c"][0].rearrange("(j p) -> p j", p=P), allow_slow_non_contiguous=True).then_inc(setup, 16)
                act.dma_start(rope[:, :, :, :], a["rope"]).then_inc(loaded, 16)
                act.wait_ge(setup, 32)
                act.wait_ge(consts, 1)
                act.activation(silu_c[:, :, 0:2], c_in[:, :, :].rearrange("p s j -> p j s"), ACT.Silu).then_inc(act_step, 1)
                act.wait_ge(act_step, 1)

            @block.gpsimd
            def _(pool):
                mine = [0]

                def step(ins):
                    mine[0] += 1
                    ins.then_inc(consts, 1)
                    pool.wait_ge(consts, mine[0])

                step(pool.memset(silu_c[:, :, :], 0.0))
                step(pool.memset(minus_half[:, :], -0.5))
                step(pool.memset(ident[:, :], 0.0))
                step(pool.affine_select(out=ident[:, :], in_=ident[:, :], compare_op=ALU.not_equal, fill=1.0,
                                        base=0, pattern=[[-1, P]], channel_multiplier=1))
                step(pool.memset(pick[:, :, :], 0.0))
                for s in range(2):
                    for g in range(4):
                        step(pool.affine_select(out=pick[:, s, :], in_=pick[:, s, :], compare_op=ALU.not_equal,
                                                fill=1.0, base=-(32 * g + s), pattern=[[0, P]], channel_multiplier=1))
                step(pool.memset(hf[:, 0, 0:2 * P], 0.0))
                step(pool.affine_select(out=hf[:, 0, 0:P], in_=hf[:, 0, 0:P], compare_op=ALU.is_ge, fill=NEG,
                                        base=0, pattern=[[1, P]], channel_multiplier=-1))
                step(pool.affine_select(out=hf[:, 0, P:2 * P], in_=hf[:, 0, P:2 * P], compare_op=ALU.is_ge, fill=NEG,
                                        base=0, pattern=[[-1, P]], channel_multiplier=1))

            @block.vector
            def _(dve):
                dve.wait_ge(consts, 16)
                dve.tensor_copy(ident_r[:, :], ident[:, :]).then_inc(dve_step, 1)
                dve.tensor_copy(mask_r[:, :, :].rearrange("p s n -> p (s n)"), hf[:, 0, 0:2 * P]).then_inc(dve_step, 1)
                dve.wait_ge(dve_step, 2)

        with nc.Fori(0, DEPTH) as layer:
            for s in per_layer:
                nc.sync.sem_clear(s)
            nc.all_engine_barrier()
            w_of = {"mod": a["w_mod"], "in": a["w_in"], "gate": a["w_gate"], "out": a["w_out"],
                    ("proj", 0): a["w_proj_a"], ("proj", 1): a["w_proj_b"], ("proj", 2): a["w_proj_c"]}
            N_UNITS_MAIN = len(UNITS)

            def of_layer(name):
                src = a[name]
                return src[(bass.ds(layer, 1),) + (slice(None),) * (len(src.shape) - 1)]

            def unit_source(kind, index, k0, nk, col, width):
                w = w_of[(kind, index) if kind == "proj" else kind]
                rows = w[bass.ds(layer, 1), k0 * P:(k0 + nk) * P, col:col + width]
                return rows.rearrange("a (k p) n -> p (a k) n", p=P)

            with nc.Block() as block:
                def normalise(act, tally, t):
                    act.wait_ge(nmr_ready, t + 1)
                    tally.did(act.activation(x[:, t, :], x[:, t, :], ACT.Identity, bias=nmr[:, t:t + 1],
                                             scale=rstd[:, t:t + 1]), x_normed)

                def apply_ln_g(dve, did, t):
                    dve.wait_ge(x_normed, t + 1)
                    did(dve.tensor_tensor(x[:, t, :], x[:, t, :], ln_g_bc[:, :], ALU.mult), x_scaled)

                def add_ln_b(pool, did, t):
                    pool.wait_ge(x_scaled, t + 1)
                    did(pool.tensor_tensor(x[:, t, :], x[:, t, :], ln_b_bc[:, :], ALU.add), x_done)
                    if t == T - 1:
                        pool.wait_ge(x_done, T)

                @block.sync
                def _(sp):
                    for n in range(N_UNITS_MAIN):
                        r, full = raw_at(n)
                        if n >= RAW:
                            m = n - RAW
                            kind, _, k0, _, col, _ = UNITS[m]
                            if kind == "mod" and k0 == 0:
                                sp.wait_ge(mod_half, col // COLS + 1)
                            elif kind == "mod":
                                wait_filled(sp, ("mod", col // COLS))
                            else:
                                sp.wait_ge(w_ready, SPLIT_UNITS.index(m) + 1)
                        sp.dma_start(raw[:, r, :].rearrange("p (k n) -> p k n", k=UNITS[n][3]),
                                     unit_source(*UNITS[n])).then_inc(raw_full[r], 16)

                @block.tensor
                def _(pe):
                    tally = Tally(pe, pe_step)

                    def begin(stage):
                        for f in FORMER[stage]:
                            if f[0] == "ot":
                                pe.wait_ge(ot_done, TILE_NO[f[1:]] + 1)
                            else:
                                wait_drained(pe, f)
                        return PLACE[stage][0]

                    def split_product(out, st_hi, st_lo, mv_hi, mv_lo, start, stop):
                        pe.matmul(out, st_hi, mv_hi, start=start, stop=False)
                        pe.matmul(out, st_hi, mv_lo, start=False, stop=False)
                        return pe.matmul(out, st_lo, mv_hi, start=False, stop=stop)

                    def ring(u, k):
                        width = UNITS[SPLIT_UNITS[u]][5]
                        cols = slice(k * width, (k + 1) * width)
                        return w_hi[:, u % RING, cols], w_lo[:, u % RING, cols]

                    def tile_product(stage, u, k_first, ready):
                        _, _, _, nk, _, width = UNITS[SPLIT_UNITS[u]]
                        t, b = stage[2], PLACE[stage][0]
                        for k in range(nk):
                            kk = k_first + k
                            if ready is not None:
                                pe.wait_ge(ready, kk + 1)
                            wh, wl = ring(u, k)
                            tok = slice(t * P, (t + 1) * P)
                            last = split_product(ps[:, b, 0:width], h_hi[:, kk, tok], h_lo[:, kk, tok], wh, wl,
                                                 kk == 0, kk == KT_D - 1)
                        return last

                    def unit_pass(name, n):
                        kind = ("out", 0) if name == "out0" else ("in", name)
                        u = USES[name][n]
                        pe.wait_ge(w_ready, u + 1)
                        ready = {"kv_a": h_ready, "out0": m_ready}.get(name)
                        nk = UNITS[SPLIT_UNITS[u]][3]
                        final = n == len(USES[name]) - 1
                        for t in range(T):
                            stage = kind + (t,)
                            if n == 0:
                                begin(stage)
                            last = tile_product(stage, u, n * nk, ready if t == 0 else None)
                            if final:
                                tally.did(last, filled[PLACE[stage][0]])
                        if not final:
                            tally.did(last, w_used)

                    def channel_rows(stage, act_hi, act_lo, kt):
                        j = stage[2]
                        s = begin(stage)
                        mine = USES[stage]
                        c = (j % 2) * P
                        for k in range(kt):
                            if j % 2 == 0 and k % UK == 0:
                                pe.wait_ge(w_ready, mine[k // UK] + 1)
                            wh, wl = ring(mine[k // UK], k % UK)
                            for part, (w, acts) in enumerate(((wh, act_hi), (wh, act_lo), (wl, act_hi))):
                                for half in range(2):
                                    last = pe.matmul(ps[:, s + half, 0:HALF], w[:, c:c + P],
                                                     acts[:, k, half * HALF:(half + 1) * HALF],
                                                     start=k == 0 and part == 0, stop=k == kt - 1 and part == 2)
                        tally.did(last, filled[s])

                    for e in ORDER:
                        kind = e[0]
                        if kind == "mod" and e[1] < 8:
                            s = begin(e)
                            for half in range(2):
                                r, full = raw_at(2 * e[1] + half)
                                pe.wait_ge(raw_full[r], full)
                                for k in range(UK):
                                    last = pe.matmul(ps[32 * k:32 * k + 32, s, 0:COLS],
                                                     silu_c[:, half * UK + k, :],
                                                     raw[:, r, k * COLS:(k + 1) * COLS],
                                                     start=half == 0, stop=half == 1)
                                tally.did(last, filled[s] if half else mod_half)
                        elif kind == "mod":
                            g = e[1] - 8
                            s = begin(e)
                            pe.wait_ge(modg_in, 32 * (g + 1))
                            for half in range(2):
                                for k in range(UK):
                                    last = pe.matmul(ps[32 * k:32 * k + 32, s, 0:COLS],
                                                     silu_c[:, half * UK + k, :], mod_raw[:, half, k, :],
                                                     start=half == 0, stop=half == 1)
                            tally.did(last, filled[s])
                        elif kind == "bc":
                            g = e[1] - 8
                            s = begin(e)
                            wait_drained(pe, ("mod", e[1]))
                            for v in range(2):
                                last = pe.matmul(ps[:, s, v * COLS:(v + 1) * COLS], pick[:, v, :], gate_rows[:, g % 2, :],
                                                 start=True, stop=True)
                            tally.did(last, filled[s])
                        elif kind == "cols":
                            s = begin(e)
                            wait_drained(pe, ("mod", 7))
                            wait_drained(pe, ("mod", 6))
                            wait_drained(pe, ("mod", 5))
                            wait_drained(pe, ("mod", 4))
                            for n in range(2 * KT_D):
                                pe.matmul(slot(s)[:, 2 * n:2 * n + 2], mod_rows[:, n * P:(n + 1) * P],
                                          pick[:, :, 0], start=True, stop=True)
                            pe.wait_ge(wsp_ready, 16)
                            for g in range(KT_B):
                                last = pe.transpose(ps[:, s + 1, g * P:(g + 1) * P], wsp_in[:, g, :], ident[:, :])
                            tally.did(last, filled[s])
                        elif kind == "h":
                            s = begin(e)
                            if e[1] == 0:
                                pe.wait_ge(xn_ready, T)
                            for t in range(T):
                                last = pe.transpose(slot(s)[:, t * P:(t + 1) * P],
                                                    xn[:, t, e[1] * P:(e[1] + 1) * P], ident[:, :])
                            tally.did(last, filled[s])
                        elif kind == "mm":
                            unit_pass(*e[1:])
                        elif kind == "kt":
                            _, br, t = e
                            s = begin(e)
                            if t < T:
                                pe.wait_ge(staged, STAGED[("k", br, t)])
                            for kv in range(NKV):
                                if t == CACHE:
                                    src = cache_k[:, "ab".index(br), kv, :, :]
                                else:
                                    src = k_st[:, k_buffer(t), kv, :, :]
                                last = pe.transpose(ps[:, s, kv * P:(kv + 1) * P],
                                                    src.rearrange("p d n -> p (d n)"), ident[:, :])
                            tally.did(last, filled[s])
                        elif kind == "qt":
                            _, br, kv, t = e
                            s = begin(e)
                            pe.wait_ge(staged, STAGED[("q", br, t)])
                            for hh in range(GRP):
                                head = kv * GRP + hh
                                last = pe.transpose(ps[0:HD, s, hh * P:(hh + 1) * P],
                                                    q_st[:, t % 3, head * HD:(head + 1) * HD], ident[:, :])
                            tally.did(last, filled[s])
                        elif kind == "s":
                            _, br, i = e
                            if i == 0:
                                for f in FORMER_OF_ATTENTION[br]:
                                    wait_drained(pe, f)
                            s = begin(e)
                            t, kv = QUERY_TILES[i // HEADS], i % HEADS // GRP
                            keys = key_slots(br, t)
                            q = q_t[:, i % HEADS, t * P:(t + 1) * P]
                            for col, width, src in key_runs(keys):
                                masks = [(n, m) for n, (_, m) in enumerate(keys) if m and col <= n * P < col + width]
                                pe.matmul(slot(s)[:, col:col + width], q, k_hi[:, kv, src:src + width],
                                          start=True, stop=False)
                                last = pe.matmul(slot(s)[:, col:col + width], q, k_lo[:, kv, src:src + width],
                                                 start=False, stop=not masks)
                                for n, m in masks:
                                    last = pe.matmul(slot(s)[:, n * P:(n + 1) * P], ident_r[:, :],
                                                     mask_r[:, 0 if m == "before" else 1, :],
                                                     start=False, stop=(n, m) == masks[-1])
                            tally.did(last, filled[s])
                        elif kind == "pt":
                            _, br, i = e
                            keys = key_slots(br, QUERY_TILES[i // HEADS])
                            wait_drained(pe, ("s", br, i))
                            na, nb = PT_COUNT[(br, i)]
                            if na:
                                pe.wait_ge(pt_a, na)
                            if nb:
                                pe.wait_ge(pt_b, nb)
                            first = pt_split(len(keys))
                            for n in range(len(keys)):
                                bank, col = (4, n) if n < first else (5, n - first)
                                last = pe.transpose(ps[:, bank, col * P:(col + 1) * P],
                                                    prob[:, i % 2, n * P:(n + 1) * P], ident[:, :])
                            tally.did(last, p_turned)
                        elif kind == "pv":
                            _, br, i = e
                            hh, kv = i % GRP, i % HEADS // GRP
                            keys = key_slots(br, QUERY_TILES[i // HEADS])
                            na, nb = PT_COUNT[(br, i)]
                            pe.wait_ge(pt_a, na + 1)
                            if len(keys) > pt_split(len(keys)):
                                pe.wait_ge(pt_b, nb + 1)
                            o = TILE_NO[(br, i // GRP)]
                            if hh == 0 and o >= 2:
                                pe.wait_ge(ot_done, o - 1)
                            for n, (ks, _) in enumerate(keys):
                                v = cache_v[:, "ab".index(br), kv * HD:(kv + 1) * HD] if ks == CACHE \
                                    else vals[:, ks, kv * HD:(kv + 1) * HD]
                                last = pe.matmul(ps[:, 6 + o % 2, hh * HD:(hh + 1) * HD], prob_t[:, i % 2, n, :], v,
                                                 start=n == 0, stop=n == len(keys) - 1)
                            tally.did(last, o_full)
                        elif kind == "ot":
                            o = TILE_NO[e[1:]]
                            pe.wait_ge(og_ready, o + 1)
                            for c in range(2):
                                last = pe.transpose(ps[:, 6 + o % 2, c * P:(c + 1) * P],
                                                    og[:, o % 2, c * P:(c + 1) * P], ident[:, :])
                            tally.did(last, ot_full)
                        elif kind == "z":
                            channel_rows(e, h_hi, h_lo, KT_D)
                        elif kind == "y":
                            if e[2] == 0:
                                if e[1] < 2:
                                    pe.wait_ge(ot_done, TILE_NO[("ab"[e[1]], NKV * T - 1)] + 1)
                                else:
                                    for g in range(KT_B):
                                        wait_drained(pe, ("ct", g))
                            channel_rows(e, o_hi, o_lo, KT_B)
                        elif kind == "mix":
                            g = e[1]
                            s = begin(e)
                            pe.wait_ge(vn_ready, T)
                            pe.matmul(slot(s)[:, 0:4 * P], w_sp_t[:, g, :], vn[:, 0:4, g * P:(g + 1) * P],
                                      start=True, stop=True)
                            last = pe.matmul(slot(s)[:, 4 * P:TOK], w_sp_t[:, g, :], vn[:, 4, g * P:(g + 1) * P],
                                             start=True, stop=True)
                            tally.did(last, filled[s])
                        elif kind == "ct":
                            g = e[1]
                            s = begin(e)
                            wait_drained(pe, ("mix", g))
                            for t in range(T):
                                last = pe.transpose(slot(s)[:, t * P:(t + 1) * P], ug[:, t, g * P:(g + 1) * P],
                                                    ident[:, :])
                            tally.did(last, filled[s])
                        elif kind == "out" and e[1] == 1:
                            begin(e)
                            for n, u in enumerate(USES["out1"]):
                                if e[2] == 0:
                                    pe.wait_ge(w_ready, u + 1)
                                last = tile_product(e, u, n * UNITS[SPLIT_UNITS[u]][3], None)
                            tally.did(last, filled[PLACE[e][0]])

                @block.scalar
                def _(act):
                    tally = Tally(act, act_step)

                    def load(sm, dst, src, by_element=False):
                        act.dma_start(dst, src, allow_slow_non_contiguous=by_element).then_inc(sm, 16)

                    load(params, b_mod_col[:, :], of_layer("b_mod")[:, 0:2 * D].rearrange("a (j p) -> p (a j)", p=P), True)
                    load(wsp_ready, wsp_in[:, :, :], of_layer("w_spatial").rearrange("a g p q -> p (a g) q"))
                    for n, name in enumerate(("q_norm", "k_norm")):
                        row = of_layer(name)
                        load(params, norm[:, n, 0, :], row.to_broadcast([P, HD]))
                        load(params, norm[:, n, 1, 0:HD // 2], row[:, HD // 2:HD].to_broadcast([P, HD // 2]))
                        load(params, norm[:, n, 1, HD // 2:HD], row[:, 0:HD // 2].to_broadcast([P, HD // 2]))
                    load(params, sink[:, :], of_layer("sink").to_broadcast([P, 2 * GRP]))
                    for n, br in enumerate("ab"):
                        keys = a[f"cache_{br}_k"][0, bass.ds(layer, 1)].rearrange("a p h d -> p (a h) d")
                        vs = a[f"cache_{br}_v"][0, bass.ds(layer, 1)].rearrange("a p h d -> p (a h d)")
                        for dup in range(2):
                            load(params, cache_k[:, n, :, dup, :], keys)
                        load(params, cache_v[:, n, :], vs)
                    load(params, b_gate_col[:, :], of_layer("b_gate").rearrange("a (j p) -> p (a j)", p=P), True)
                    load(params, b_sp_col[:, :], of_layer("b_spatial").rearrange("a g p -> p (a g)"), True)

                    def split_hi(n):
                        m = SPLIT_UNITS[n]
                        r, full = raw_at(m)
                        act.wait_ge(raw_full[r], full)
                        if n >= RING:
                            last = LAST_USE[n - RING]
                            if last in W_USED_NO:
                                act.wait_ge(w_used, W_USED_NO[last])
                            elif last[0] in ("in", "out") and last[1] != 1:
                                wait_filled(act, last[:2] + (T - 1,))
                            else:
                                wait_filled(act, last)
                        tally.did(act.activation(w_hi[:, n % RING, :], raw[:, r, :], ACT.Copy), hi_made)

                    pt_b_done = 0
                    for e in ORDER:
                        kind = e[0]
                        if kind == "split":
                            split_hi(e[1])
                        elif kind == "mod" and e[1] >= 8:
                            g = e[1] - 8
                            if g < 3:
                                wait_filled(act, e)
                                for half in range(2):
                                    load(modg_in, mod_raw[:, half, :, :],
                                         unit_source("mod", 0, half * UK, UK, (9 + g) * COLS, COLS))
                        elif kind == "h":
                            wait_drained(act, e)
                            tally.did(act.activation(h_hi[:, e[1], :], hf[:, e[1] % 2, :], ACT.Copy), hh_ready)
                        elif kind == "in":
                            _, name, t = e
                            if name in ("kv_a", "q_a"):
                                s = wait_filled(act, e)
                                n = SQ_NO[e]
                                if n >= 2:
                                    act.wait_ge(staged, SQ_STAGED[n - 2])
                                w = P if name == "kv_a" else BW
                                tally.did(act.activation(square[:, n % 2, 0:w], ps[:, s, 0:w], ACT.Square), sq_ready)
                            elif name in ("g_a", "g_b", "g_c"):
                                s = wait_filled(act, e)
                                dst = ug if name == "g_c" else gate_br
                                tally.did(act.activation(dst[:, t, :], ps[:, s, :], ACT.Silu), drained[s])
                            elif name == "v_c":
                                s = wait_filled(act, e)
                                if t == 0:
                                    load(late, sgu_g[:, :], of_layer("sgu_g").to_broadcast([P, BW]))
                                    load(late, sgu_b[:, :], of_layer("sgu_b").to_broadcast([P, BW]))
                                tally.did(act.activation(vn[:, t, :], ps[:, s, :], ACT.Copy), drained[s])
                        elif kind == "kt":
                            s = wait_filled(act, e)
                            _, br, t = e
                            tally.did(act.activation(k_hi[:, :, t * P:(t + 1) * P],
                                                     ps[:, s, 0:2 * P].rearrange("p (v n) -> p v n", v=NKV), ACT.Copy),
                                      t_hi)
                            if t == CACHE:
                                act.wait_ge(staged, STAGED[("k", br, 0)])
                                load(state_out, outs[f"state_{br}_k"][0, bass.ds(layer, 1)].rearrange("a p h d -> p (a h) d"),
                                     k_st[:, 0, :, 0, :])
                                load(state_out, outs[f"state_{br}_v"][0, bass.ds(layer, 1)].rearrange("a p h d -> p (a h d)"),
                                     vals[:, 0, :])
                        elif kind == "qt":
                            s = wait_filled(act, e)
                            _, br, kv, t = e
                            scale = 1.0 if br == "a" else HD ** -0.5
                            tally.did(act.activation(q_t[0:HD, kv * GRP:(kv + 1) * GRP, t * P:(t + 1) * P],
                                                     ps[0:HD, s, :].rearrange("p (h n) -> p h n", h=GRP),
                                                     ACT.Copy, scale=scale), t_hi)
                        elif kind == "s":
                            _, br, i = e
                            n = len(key_slots(br, QUERY_TILES[i // HEADS])) * P
                            u = UNIT_NO[(br, i)]
                            s = wait_filled(act, e)
                            act.wait_ge(nm_ready, u + 1)
                            if i >= 2:
                                act.wait_ge(p_turned, u - 1)
                            c = u % 8
                            tally.did(act.activation(prob[:, i % 2, 0:n], slot(s)[:, 0:n], ACT.Exp,
                                                     bias=neg_top[:, c:c + 1], accum_out=psums[:, c:c + 1]), drained[s])
                            if br == "b":
                                head = i % HEADS
                                tally.did(act.activation(psink[:, c:c + 1], sink[:, head:head + 1], ACT.Exp,
                                                         bias=neg_top[:, c:c + 1]), sink_exp)
                        elif kind == "pt":
                            _, br, i = e
                            nk = len(key_slots(br, QUERY_TILES[i // HEADS]))
                            first = pt_split(nk)
                            if nk > first:
                                u = UNIT_NO[(br, i)]
                                act.wait_ge(p_turned, u + 1)
                                if i >= 2:
                                    act.wait_ge(o_full, u - 1)
                                tally.did(act.activation(prob_t[:, i % 2, first:nk, :].rearrange("p k n -> p (k n)"),
                                                         ps[:, 5, 0:(nk - first) * P], ACT.Copy), pt_b)
                        elif kind == "ot":
                            _, br, j = e
                            o = TILE_NO[(br, j)]
                            t, kv = QUERY_TILES[j // NKV], j % NKV
                            act.wait_ge(ot_full, o + 1)
                            tally.did(act.activation(o_hi[:, 2 * kv:2 * kv + 2, t * P:(t + 1) * P],
                                                     ps[:, 6 + o % 2, 0:2 * P].rearrange("p (c n) -> p c n", c=2), ACT.Copy),
                                      t_hi)
                        elif kind == "z":
                            _, r, j = e
                            s = wait_filled(act, e)
                            n = r * KT_D + j
                            if n >= 2:
                                wait_drained(act, ("y", (n - 2) // KT_D, (n - 2) % KT_D))
                            tally.did(act.activation(sg[:, j % 2, :].rearrange("p (b n) -> p b n", b=2),
                                                     ps[:, s:s + 2, 0:HALF], ACT.Sigmoid,
                                                     bias=b_gate_col[:, n:n + 1]), drained[s])
                            if r == 2 and j == 0:
                                for half in range(2):
                                    load(modg_in, mod_raw[:, half, :, :], unit_source("mod", 0, half * UK, UK, 8 * COLS, COLS))
                                load(ends, b_modg_bc[:, :], of_layer("b_mod")[:, 2 * D:3 * D].to_broadcast([P, D]))
                                load(ends, ln_g_bc[:, :], of_layer("ln_g").to_broadcast([P, D]))
                                load(ends, ln_b_bc[:, :], of_layer("ln_b").to_broadcast([P, D]))
                        elif kind == "ct":
                            g = e[1]
                            s = wait_filled(act, e)
                            tally.did(act.activation(o_hi[:, g, :], slot(s)[:, 0:TOK], ACT.Copy), t_hi)
                        elif kind == "m":
                            j = e[1]
                            act.wait_ge(merged, KT_D + j + 1)
                            if j == 0:
                                wait_filled(act, ("z", 2, KT_D - 1))
                            tally.did(act.activation(h_hi[:, j, :], merge[:, j, :], ACT.Copy), m_hi)
                        elif kind == "out" and e[1] == 1:
                            if e[2] >= 1:
                                normalise(act, tally, e[2] - 1)
                    normalise(act, tally, T - 1)
                    act.wait_ge(state_out, 64)

                @block.vector
                def _(dve):
                    tally = Tally(dve, dve_step)
                    did = tally.did
                    rstds = [0]
                    outs_seen = [0]

                    def after(token):
                        dve.wait_ge(*token)

                    def ask_rstd(instruction):
                        return did(instruction, var_ready)

                    def await_rstd():
                        rstds[0] += 1
                        dve.wait_ge(rstd_ready, rstds[0])

                    def moments(t, halves):
                        for n, src in enumerate(halves):
                            tok = did(dve.bn_stats(bn[:, t, n, :], src))
                        after(tok)
                        return dve.bn_aggr(mv[:, t, :], bn[:, t, 0:len(halves), :])

                    def drain(instruction, stage):
                        did(instruction, drained[PLACE[stage][0]])
                        wait_drained(dve, stage)

                    def rotate(dst, src, tab, heads, dup, stage):
                        half = HD // 2
                        rc = rot_c[:, 0:heads * HD].rearrange("p (h d) -> p h d", h=heads)
                        rs = rot_s[:, 0:heads * HD].rearrange("p (h d) -> p h d", h=heads)
                        did(dve.tensor_tensor(rc, src, tab[:, 0:1, :].to_broadcast([P, heads, HD]), ALU.mult))
                        did(dve.tensor_tensor(rs[:, :, 0:half], src[:, :, half:HD],
                                              tab[:, 1:2, 0:half].to_broadcast([P, heads, half]), ALU.mult))
                        last = dve.tensor_tensor(rs[:, :, half:HD], src[:, :, 0:half],
                                                 tab[:, 1:2, half:HD].to_broadcast([P, heads, half]), ALU.mult)
                        if stage is None:
                            after(did(last))
                        else:
                            drain(last, stage)
                        if dup:
                            rc = rc.unsqueeze(2).to_broadcast([P, heads, 2, HD])
                            rs = rs.unsqueeze(2).to_broadcast([P, heads, 2, HD])
                        did(dve.tensor_tensor(dst, rc, rs, ALU.add), staged)

                    def queries_or_keys(e, br, is_key):
                        _, _, t = e
                        s = wait_filled(dve, e)
                        heads = NKV if is_key else HEADS
                        src = ps[:, s, 0:heads * HD].rearrange("p (h d) -> p h d", h=heads)
                        if br == "a":
                            dve.wait_ge(sq_ready, SQ_NO[e] + 1)
                        if is_key and br == "b" and t == 0:
                            dve.wait_ge(state_out, 32)
                            for j in (KT_D - 2, KT_D - 1):
                                wait_drained(dve, ("y", 0, j))
                        if is_key:
                            did(dve.tensor_copy(vals[:, t, :], ps[:, s, P:2 * P]))
                            dst = k_st[:, k_buffer(t), :, :, :]
                        else:
                            dst = q_st[:, t % 3, :].rearrange("p (h d) -> p h d", h=heads)
                        if is_key and t >= 3:
                            wait_filled(dve, ("kt", br, t - 2))
                        if not is_key and t >= 3:
                            wait_filled(dve, ("qt", br, NKV - 1, t - 3))
                        stage = e
                        if tally.count(staged):
                            dve.wait_ge(staged, tally.count(staged))
                        if br == "a":
                            c = SQ_NO[e] % 2
                            ask_rstd(dve.tensor_reduce(ssq[:, c, 0:heads],
                                                       square[:, c, 0:heads * HD].rearrange("p (h d) -> p h d", h=heads),
                                                       axis=AX.X, op=ALU.add))
                            await_rstd()
                            flat = square[:, c, 0:heads * HD].rearrange("p (h d) -> p h d", h=heads)
                            drain(dve.tensor_tensor(flat, src, rqk[:, c, 0:heads].unsqueeze(2).to_broadcast([P, heads, HD]),
                                                    ALU.mult), e)
                            src, stage = flat, None
                        tab = 1 if is_key else 0
                        if t > 0:
                            w = table[:, tab, t - 1, :, :] if br == "a" else rope[:, t - 1, :, :]
                            rotate(dst, src, w, heads, is_key, stage)
                        elif br == "a":
                            w = norm[:, tab, 0:1, :]
                            if is_key:
                                did(dve.tensor_tensor(dst, src.unsqueeze(2).to_broadcast([P, heads, 2, HD]),
                                                      w.unsqueeze(2).to_broadcast([P, heads, 2, HD]), ALU.mult), staged)
                            else:
                                did(dve.tensor_tensor(dst, src, w.to_broadcast([P, heads, HD]), ALU.mult), staged)
                        else:
                            c = rot_c[:, 0:heads * HD].rearrange("p (h d) -> p h d", h=heads)
                            drain(dve.tensor_copy(c, src), e)
                            if is_key:
                                c = c.unsqueeze(2).to_broadcast([P, heads, 2, HD])
                            did(dve.tensor_copy(dst, c), staged)

                    dve.wait_ge(loaded, 16 * (T + 1))
                    for t in range(T):
                        tok = did(moments(t, [x[:, t, 0:512], x[:, t, 512:D]]))
                    after(tok)
                    ask_rstd(dve.tensor_copy(rstd[:, :], mv[:, :, 1]))
                    await_rstd()
                    for t in range(T):
                        did(dve.tensor_scalar(xn[:, t, :], x[:, t, :], mv[:, t, 0:1], rstd[:, t:t + 1],
                                              ALU.subtract, ALU.mult), xn_ready)
                    dve.wait_ge(params, 16 * PARAM_LOADS)
                    after(did(dve.tensor_scalar(norm[:, 1, :, :], norm[:, 1, :, :], float(HD) ** 0.5, None, ALU.mult)))
                    for n in range(2):
                        did(dve.tensor_tensor(table[:, n, :, :, :].rearrange("p t c d -> p t (c d)"),
                                              rope[:, :, :, :].rearrange("p t c d -> p t (c d)"),
                                              norm[:, n, :, :].rearrange("p c d -> p (c d)").unsqueeze(1)
                                              .to_broadcast([P, T - 1, 2 * HD]), ALU.mult))

                    for e in ORDER:
                        kind = e[0]
                        if kind == "mod":
                            s = wait_filled(dve, e)
                            if e[1] < 8:
                                did(dve.tensor_copy(mod_rows[:, e[1] * COLS:(e[1] + 1) * COLS], ps[:, s, 0:COLS]),
                                    drained[s])
                            else:
                                g = e[1] - 8
                                did(dve.tensor_copy(gate_rows[:, g % 2, :], ps[:, s, 0:COLS]), drained[s])
                        elif kind == "bc":
                            g = e[1] - 8
                            s = wait_filled(dve, e)
                            if g == 0:
                                dve.wait_ge(ends, 48)
                            cols = slice(g * COLS, (g + 1) * COLS)
                            did(dve.tensor_tensor(gate_bc[:, :, cols], ps[:, s, :].rearrange("p (v n) -> p v n", v=2),
                                                  b_modg_bc[:, cols].unsqueeze(1).to_broadcast([P, 2, COLS]), ALU.add),
                                drained[s])
                        elif kind == "cols":
                            s = wait_filled(dve, e)
                            cols = slot(s)[:, 0:4 * KT_D].rearrange("p (j v) -> p j v", v=2)
                            bias = b_mod_col[:, :].unsqueeze(2).to_broadcast([P, 2 * KT_D, 2])
                            after(did(dve.tensor_tensor(ada[:, :, :], cols, bias, ALU.add)))
                            did(dve.tensor_scalar(ada[:, KT_D:, :], ada[:, KT_D:, :], 1.0, None, ALU.add))
                            drain(dve.tensor_copy(w_sp_t[:, :, :].rearrange("p g n -> p (g n)"), ps[:, s + 1, :]), e)
                        elif kind == "h":
                            j = e[1]
                            s = wait_filled(dve, e)
                            if j >= 2:
                                dve.wait_ge(h_ready, j - 1)
                            did(dve.tensor_scalar(hf[:, j % 2, 0:P], slot(s)[:, 0:P], ada[:, KT_D + j, 0:1],
                                                        ada[:, j, 0:1], ALU.mult, ALU.add))
                            did(dve.tensor_scalar(hf[:, j % 2, P:TOK], slot(s)[:, P:TOK], ada[:, KT_D + j, 1:2],
                                                  ada[:, j, 1:2], ALU.mult, ALU.add), drained[s])
                            dve.wait_ge(hh_ready, j + 1)
                            did(dve.tensor_tensor(h_lo[:, j, :], hf[:, j % 2, :], h_hi[:, j, :], ALU.subtract), h_ready)
                        elif kind == "in":
                            _, name, t = e
                            if name[0] in "kq":
                                queries_or_keys(e, name[-1], name[0] == "k")
                            elif name == "v_c":
                                wait_drained(dve, e)
                                after(did(dve.bn_stats(bn[:, t, 0, :], vn[:, t, :])))
                                tok = did(dve.bn_aggr(mv[:, t, :], bn[:, t, 0, :]))
                                if t == T - 1:
                                    after(tok)
                                    ask_rstd(dve.tensor_copy(rstd[:, :], mv[:, :, 1]))
                                    await_rstd()
                                    dve.wait_ge(late, 32)
                                    for q in range(T):
                                        after(did(dve.tensor_scalar(vn[:, q, :], vn[:, q, :], mv[:, q, 0:1],
                                                                    rstd[:, q:q + 1], ALU.subtract, ALU.mult)))
                                        after(did(dve.tensor_tensor(vn[:, q, :], vn[:, q, :], sgu_g[:, :], ALU.mult)))
                                        did(dve.tensor_tensor(vn[:, q, :], vn[:, q, :], sgu_b[:, :], ALU.add), vn_ready)
                            elif name == "u_c":
                                s = wait_filled(dve, e)
                                wait_drained(dve, ("in", "g_c", t))
                                did(dve.tensor_tensor(ug[:, t, :], ps[:, s, :], ug[:, t, :], ALU.mult), drained[s])
                        elif kind == "kt":
                            _, br, t = e
                            s = wait_filled(dve, e)
                            dve.wait_ge(t_hi, T_HI_NO[e])
                            did(dve.tensor_tensor(k_lo[:, :, t * P:(t + 1) * P],
                                                  ps[:, s, 0:2 * P].rearrange("p (v n) -> p v n", v=NKV),
                                                  k_hi[:, :, t * P:(t + 1) * P], ALU.subtract), drained[s])
                        elif kind == "qt":
                            _, br, kv, t = e
                            s = wait_filled(dve, e)
                            dve.wait_ge(t_hi, T_HI_NO[e])
                            scale = 1.0 if br == "a" else HD ** -0.5
                            heads = slice(kv * GRP, (kv + 1) * GRP)
                            did(dve.scalar_tensor_tensor(q_t[HD:P, heads, t * P:(t + 1) * P],
                                                         ps[0:HD, s, :].rearrange("p (h n) -> p h n", h=GRP), scale,
                                                         q_t[0:HD, heads, t * P:(t + 1) * P], ALU.mult, ALU.subtract),
                                drained[s])
                        elif kind == "s":
                            _, br, i = e
                            n = len(key_slots(br, QUERY_TILES[i // HEADS])) * P
                            u = UNIT_NO[(br, i)]
                            c = u % 8
                            s = wait_filled(dve, e)
                            after(did(dve.tensor_reduce(top[:, c:c + 1], slot(s)[:, 0:n], axis=AX.X, op=ALU.max)))
                            if br == "a":
                                did(dve.tensor_scalar(neg_top[:, c:c + 1], top[:, c:c + 1], -1.0, None, ALU.mult), nm_ready)
                            else:
                                head = i % HEADS
                                did(dve.tensor_scalar(neg_top[:, c:c + 1], top[:, c:c + 1], sink[:, head:head + 1], -1.0,
                                                      ALU.max, ALU.mult), nm_ready)
                        elif kind == "pt":
                            _, br, i = e
                            first = pt_split(len(key_slots(br, QUERY_TILES[i // HEADS])))
                            u = UNIT_NO[(br, i)]
                            dve.wait_ge(p_turned, u + 1)
                            if i >= 2:
                                dve.wait_ge(o_full, u - 1)
                            did(dve.tensor_copy(prob_t[:, i % 2, 0:first, :].rearrange("p k n -> p (k n)"),
                                                ps[:, 4, 0:first * P]), pt_a)
                        elif kind == "pv" and e[2] % GRP == GRP - 1:
                            _, br, i = e
                            u = UNIT_NO[(br, i)]
                            o = TILE_NO[(br, i // GRP)]
                            t, kv = QUERY_TILES[i // HEADS], i % HEADS // GRP
                            c0 = (u - 3) % 8
                            den = psums[:, c0:c0 + GRP]
                            ro = rinv[:, o % 2, :]
                            wait_drained(dve, ("s", br, i))
                            if br == "b":
                                dve.wait_ge(sink_exp, u + 1 - SINK_FIRST)
                                after(did(dve.tensor_tensor(den, den, psink[:, c0:c0 + GRP], ALU.add)))
                            after(did(dve.reciprocal(ro, den)))
                            if o >= 2:
                                dve.wait_ge(ot_full, o - 1)
                            dve.wait_ge(o_full, u + 1)
                            dst = og[:, o % 2, :].rearrange("p (h d) -> p h d", h=GRP)
                            after(did(dve.tensor_tensor(dst, ps[:, 6 + o % 2, 0:COLS].rearrange("p (h d) -> p h d", h=GRP),
                                                        ro.unsqueeze(2).to_broadcast([P, GRP, HD]), ALU.mult)))
                            did(dve.tensor_tensor(og[:, o % 2, :], og[:, o % 2, :],
                                                  gate_br[:, t, kv * COLS:(kv + 1) * COLS], ALU.mult), og_ready)
                        elif kind == "ot":
                            _, br, j = e
                            o = TILE_NO[(br, j)]
                            t, kv = QUERY_TILES[j // NKV], j % NKV
                            dve.wait_ge(t_hi, T_HI_NO[e])
                            dst = slice(2 * kv, 2 * kv + 2), slice(t * P, (t + 1) * P)
                            did(dve.tensor_tensor(o_lo[:, dst[0], dst[1]],
                                                  ps[:, 6 + o % 2, 0:2 * P].rearrange("p (c n) -> p c n", c=2),
                                                  o_hi[:, dst[0], dst[1]], ALU.subtract), ot_done)
                        elif kind == "y":
                            _, r, j = e
                            s = wait_filled(dve, e)
                            wait_drained(dve, ("z", r, j))
                            y = ps[:, s:s + 2, 0:HALF]
                            g2 = sg[:, j % 2, :].rearrange("p (b n) -> p b n", b=2)
                            if r == 0:
                                did(dve.tensor_tensor(merge[:, j, :].rearrange("p (b n) -> p b n", b=2), y, g2, ALU.mult),
                                    drained[s])
                            else:
                                n = (r - 1) * KT_D + j
                                if n >= 2:
                                    dve.wait_ge(merged, n - 1)
                                did(dve.tensor_tensor(gy[:, j % 2, :].rearrange("p (b n) -> p b n", b=2), y, g2, ALU.mult),
                                    drained[s])
                        elif kind == "mix":
                            g = e[1]
                            s = wait_filled(dve, e)
                            if g == 0:
                                for t in range(T):
                                    wait_drained(dve, ("in", "u_c", t))
                            did(dve.scalar_tensor_tensor(ug[:, :, g * P:(g + 1) * P],
                                                         slot(s)[:, 0:TOK].rearrange("p (t n) -> p t n", t=T),
                                                         b_sp_col[:, g:g + 1], ug[:, :, g * P:(g + 1) * P],
                                                         ALU.add, ALU.mult), drained[s])
                        elif kind == "ct":
                            g = e[1]
                            s = wait_filled(dve, e)
                            dve.wait_ge(t_hi, T_HI_NO[e])
                            did(dve.tensor_tensor(o_lo[:, g, :], slot(s)[:, 0:TOK], o_hi[:, g, :], ALU.subtract), drained[s])
                        elif kind == "m":
                            j = e[1]
                            dve.wait_ge(m_hi, j + 1)
                            did(dve.tensor_tensor(h_lo[:, j, :], merge[:, j, :], h_hi[:, j, :], ALU.subtract), m_ready)
                        elif kind == "out":
                            _, g, t = e
                            s = wait_filled(dve, e)
                            n = outs_seen[0]
                            outs_seen[0] += 1
                            cols = slice(g * BW, (g + 1) * BW)
                            drain(dve.tensor_tensor(scaled[:, n % 2, :], ps[:, s, :],
                                                    gate_bc[:, min(t, 1), cols], ALU.mult), e)
                            tok = did(dve.scalar_tensor_tensor(x[:, t, cols], x[:, t, cols], ALPHA, scaled[:, n % 2, :],
                                                               ALU.mult, ALU.add))
                            if g == 1:
                                after(tok)
                                tok = ask_rstd(moments(t, [x[:, t, 0:512], x[:, t, 512:D]]))
                                after(tok)
                                await_rstd()
                                did(dve.scalar_tensor_tensor(nmr[:, t:t + 1], mv[:, t, 0:1], -1.0, rstd[:, t:t + 1],
                                                             ALU.mult, ALU.mult), nmr_ready)
                                if t >= 1:
                                    apply_ln_g(dve, did, t - 1)
                    apply_ln_g(dve, did, T - 1)

                @block.gpsimd
                def _(pool):
                    tally = Tally(pool, pool_step)
                    did = tally.did
                    asked = [0]

                    def root(out, src, eps):
                        asked[0] += 1
                        pool.wait_ge(var_ready, asked[0])
                        n = out.shape[-1]
                        pool.wait_ge(*did(pool.tensor_scalar(with_eps[:, 0:n], src, eps, None, ALU.add)))
                        did(pool.tensor_tensor(out, with_eps[:, 0:n], minus_half[:, 0:n], ALU.pow), rstd_ready)

                    root(rstd[:, :], rstd[:, :], EPS)
                    for e in ORDER:
                        kind = e[0]
                        if kind == "split":
                            n = e[1]
                            r, _ = raw_at(SPLIT_UNITS[n])
                            pool.wait_ge(hi_made, n + 1)
                            did(pool.tensor_tensor(w_lo[:, n % RING, :], raw[:, r, :], w_hi[:, n % RING, :],
                                                   ALU.subtract), w_ready)
                        elif kind == "in" and e in SQ_NO:
                            heads = NKV if e[1] == "kv_a" else HEADS
                            c = SQ_NO[e] % 2
                            root(rqk[:, c, 0:heads], ssq[:, c, 0:heads], HD * EPS)
                        elif kind == "in" and e[1:] == ("v_c", T - 1):
                            root(rstd[:, :], rstd[:, :], EPS)
                        elif kind == "y" and e[1] >= 1:
                            _, r, j = e
                            wait_drained(pool, e)
                            did(pool.tensor_tensor(merge[:, j, :], merge[:, j, :], gy[:, j % 2, :], ALU.add), merged)
                        elif kind == "out" and e[1] == 1:
                            t = e[2]
                            root(rstd[:, t:t + 1], mv[:, t, 1:2], EPS)
                            if t >= 1:
                                add_ln_b(pool, did, t - 1)
                    add_ln_b(pool, did, T - 1)

        with nc.Block() as block:
            @block.sync
            def _(sp):
                sp.dma_start(outs["y_prompt"][0], x[:, 0, :]).then_inc(final, 16)
                for t in range(1, T):
                    sp.dma_start(outs["y_sample"][0, (t - 1) * P:t * P, :], x[:, t, :]).then_inc(final, 16)
                sp.wait_ge(final, 16 * T)


def k_buffer(t):
    return 0 if t == 0 else 1 + (t - 1) % 2


def pt_split(n):
    return {1: 1, 3: 2, 4: 2, 5: 3}[n]


def key_runs(keys):
    runs = []
    for n, (s, _) in enumerate(keys):
        if runs and runs[-1][2] + runs[-1][1] == s * P and runs[-1][1] < 512:
            runs[-1][1] += P
        else:
            runs.append([n * P, P, s * P])
    return runs


def numbers():
    staged, sq, sq_staged, t_hi, unit, tile, pt, w_used, before = {}, {}, [], {}, {}, {}, {}, {}, {}
    n_a = n_b = 0
    latest = {}
    for e in ORDER:
        if e[0] == "in" and e[1][0] in "kq":
            _, name, t = e
            staged[(name[0], name[-1], t)] = len(staged) + 1
            if name[-1] == "a":
                sq[e] = len(sq)
                sq_staged.append(len(staged))
        elif e[0] == "mm":
            if e[2] < len(USES[e[1]]) - 1:
                w_used[e] = len(w_used) + 1
        elif e[0] == "s":
            if e[2] == 0:
                before[e[1]] = sorted(set(latest.values()), key=str)
            unit[e[1:]] = len(unit)
            if e[2] % GRP == 0:
                tile[(e[1], e[2] // GRP)] = len(tile)
        elif e[0] == "pt":
            pt[e[1:]] = (n_a, n_b)
            nk = len(key_slots(e[1], QUERY_TILES[e[2] // HEADS]))
            n_a += 1
            n_b += nk > pt_split(nk)
        if e[0] in ("kt", "qt", "ct", "ot"):
            t_hi[e] = len(t_hi) + 1
        if e in PLACE:
            latest[PLACE[e][0]] = e
    return staged, sq, sq_staged, t_hi, unit, tile, pt, w_used, before


STAGED, SQ_NO, SQ_STAGED, T_HI_NO, UNIT_NO, TILE_NO, PT_COUNT, W_USED_NO, FORMER_OF_ATTENTION = numbers()
SINK_FIRST = UNIT_NO[("b", 0)]
PARAM_LOADS = 1 + 6 + 1 + 6 + 2

_INS = ['x_prompt', 'x_sample', 'cache_a_k', 'cache_a_v', 'cache_b_k', 'cache_b_v', 'c', 'c_ctx', 'w_mod', 'b_mod',
        'w_in', 'q_norm', 'k_norm', 'sink', 'sgu_g', 'sgu_b', 'w_spatial', 'b_spatial', 'w_proj_a', 'w_proj_b',
        'w_proj_c', 'w_gate', 'b_gate', 'w_out', 'ln_g', 'ln_b']
_OUTS = {"y_prompt": (1, P, D), "y_sample": (1, 4 * P, D), "state_a_k": (1, DEPTH, P, NKV, HD),
         "state_a_v": (1, DEPTH, P, NKV, HD), "state_b_k": (1, DEPTH, P, NKV, HD), "state_b_v": (1, DEPTH, P, NKV, HD)}


def rope_constants():
    grid_w, freqs, n = 64, HD // 4, 4 * P
    row = np.repeat(np.arange(n // grid_w, dtype=np.float32), grid_w)
    col = np.tile(np.arange(grid_w, dtype=np.float32), n // grid_w)
    inv = np.power(np.float32(10000.0), -np.arange(freqs, dtype=np.float32) / np.float32(freqs))
    ang = np.concatenate([row[:, None] * inv, col[:, None] * inv], axis=-1)
    c, s = np.cos(ang), np.sin(ang)
    both = np.stack([np.concatenate([c, c], -1), np.concatenate([-s, s], -1)], axis=1)
    return np.ascontiguousarray(both.reshape(4, P, 2, HD).transpose(1, 0, 2, 3)).astype(np.float32)


def kernel(**inputs):
    import concourse.bacc as _bacc
    from concourse.bass_utils import run_bass_kernel_spmd as _run

    nc = _bacc.Bacc("TRN2", target_bir_lowering=False, num_devices=1,
                     dynamic_dma_scratch_size=1024)
    arrays, args, outs = {}, {}, {}
    for name in _INS:
        v = np.ascontiguousarray(inputs[name])
        arrays[f"in_{name}"] = v
        args[name] = nc.dram_tensor(f"in_{name}", v.shape, mybir.dt.from_np(v.dtype), kind="ExternalInput").ap()
    arrays["rope_table"] = rope_constants()
    args["rope"] = nc.dram_tensor("rope_table", (P, T - 1, 2, HD), F32, kind="ExternalInput").ap()
    for name, shape in _OUTS.items():
        outs[name] = nc.dram_tensor(name, shape, F32, kind="ExternalOutput").ap()
    build(nc, args, outs)
    r = _run(nc, [arrays], core_ids=[0])
    return tuple(r.results[0][name] for name in _OUTS)
```
